# Optimizing a Trainium2 kernel written in Bass

```python
import math
import jax
import jax.numpy as jnp
from jax import lax
import numpy as np

D_MODEL = 1024
BATCH = 1
SEQ = 256
DEPTH = 2

CHUNK = 64
Q_BLOCK = 128
NORM_EPS = 1e-6
MAX_STREAM_OFFSET = 4096

GDN_HEADS = 8
GDN_DK = 128
GDN_DV = 128
CONV_WIDTH = 4
GDN_QKV = 2 * GDN_HEADS * GDN_DK + GDN_HEADS * GDN_DV
GDN_Z = GDN_HEADS * GDN_DV

MLA_HEADS = 8
MLA_Q_LORA = 384
MLA_KV_LORA = 256
MLA_NOPE = 128
MLA_ROPE = 64
MLA_V = 128
MLA_QK_DIM = MLA_NOPE + MLA_ROPE
ROPE_BASE = 10000.0

D_FF = 4 * D_MODEL

N_BRANCHES = 2
PROJ_SIZES = (GDN_QKV, GDN_Z, GDN_HEADS, GDN_HEADS, MLA_Q_LORA, MLA_KV_LORA, MLA_ROPE, N_BRANCHES * D_MODEL)
PROJ_WIDTH = GDN_QKV + GDN_Z + 2 * GDN_HEADS + MLA_Q_LORA + MLA_KV_LORA + MLA_ROPE + N_BRANCHES * D_MODEL

kernel_name = "hybrid_gdn_mla_sandwich_trunk"

def _rms_norm(x, w):
    xf = x.astype(jnp.float32)
    y = xf * lax.rsqrt(jnp.mean(xf * xf, axis=-1, keepdims=True) + NORM_EPS)
    return (y * w.astype(jnp.float32)).astype(x.dtype)

def _l2_norm(x):
    return x * lax.rsqrt(jnp.sum(x * x, axis=-1, keepdims=True) + NORM_EPS)

def _split_cols(t, sizes):
    outs, start = [], 0
    for s in sizes:
        outs.append(t[..., start:start + s])
        start += s
    return outs

def _causal_conv(x, w):
    s = x.shape[1]
    xp = jnp.pad(x, ((0, 0), (CONV_WIDTH - 1, 0), (0, 0)))
    out = xp[:, 0:s] * w[0]
    for j in range(1, CONV_WIDTH):
        out = out + xp[:, j:j + s] * w[j]
    return out

def _rope(x, cos, sin):
    half = x.shape[-1] // 2
    x1, x2 = x[..., :half], x[..., half:]
    return jnp.concatenate([x1 * cos - x2 * sin, x2 * cos + x1 * sin], axis=-1)

def _gated_delta_rule(q, k, v, g, beta):
    out_dtype = v.dtype
    q, k, v, g, beta = (t.astype(jnp.float32) for t in (q, k, v, g, beta))
    b, s, h, dk = q.shape
    dv = v.shape[-1]
    n = s // CHUNK
    q = q * dk ** -0.5
    to_chunks = lambda t: t.reshape(b, n, CHUNK, h, t.shape[-1]).transpose(0, 3, 1, 2, 4)
    q, k, v = to_chunks(q), to_chunks(k), to_chunks(v)
    g = g.reshape(b, n, CHUNK, h).transpose(0, 3, 1, 2)
    beta = beta.reshape(b, n, CHUNK, h).transpose(0, 3, 1, 2)
    gc = jnp.cumsum(g, axis=-1)
    idx = jnp.arange(CHUNK)
    incl = idx[:, None] >= idx[None, :]
    strict = idx[:, None] > idx[None, :]
    decay = jnp.exp(jnp.where(incl, gc[..., :, None] - gc[..., None, :], -jnp.inf))
    kb = k * beta[..., None]
    vb = v * beta[..., None]
    kk = jnp.einsum('bhncd,bhnmd->bhncm', kb, k) * decay
    lower = jnp.where(strict, kk, 0.0) + jnp.eye(CHUNK, dtype=kk.dtype)
    rhs = jnp.concatenate([vb, kb * jnp.exp(gc)[..., None]], axis=-1)
    sol = lax.linalg.triangular_solve(lower, rhs, left_side=True, lower=True, unit_diagonal=True)
    u, w = sol[..., :dv], sol[..., dv:]
    qk = jnp.einsum('bhncd,bhnmd->bhncm', q, k) * decay
    q_decay = q * jnp.exp(gc)[..., None]
    k_to_end = k * jnp.exp(gc[..., -1:] - gc)[..., None]
    g_end = jnp.exp(gc[..., -1])
    xs = tuple(jnp.moveaxis(t, 2, 0) for t in (qk, q_decay, k_to_end, u, w, g_end))

    def step(state, inp):
        qk_i, qd_i, kend_i, u_i, w_i, gend_i = inp
        v_new = u_i - jnp.einsum('bhck,bhkv->bhcv', w_i, state)
        o = jnp.einsum('bhck,bhkv->bhcv', qd_i, state) + jnp.einsum('bhcm,bhmv->bhcv', qk_i, v_new)
        state = state * gend_i[..., None, None] + jnp.einsum('bhck,bhcv->bhkv', kend_i, v_new)
        return state, o

    state0 = jnp.zeros((b, h, dk, dv), jnp.float32)
    _, o = lax.scan(step, state0, xs)
    o = o.transpose(1, 0, 3, 2, 4).reshape(b, s, h, dv)
    return o.astype(out_dtype)

def _chunk_causal_attention(q, k, v):
    b, s, h, dq = q.shape
    dv = v.shape[-1]
    nb = s // Q_BLOCK
    scale = dq ** -0.5
    k_chunk = jnp.arange(s) // CHUNK
    q_blocks = q.reshape(b, nb, Q_BLOCK, h, dq).transpose(1, 0, 2, 3, 4)

    def attend(args):
        qb, blk = args
        scores = jnp.einsum('bqhd,bkhd->bhqk', qb, k).astype(jnp.float32) * scale
        q_chunk = (blk * Q_BLOCK + jnp.arange(Q_BLOCK)) // CHUNK
        mask = k_chunk[None, :] <= q_chunk[:, None]
        p = jax.nn.softmax(jnp.where(mask, scores, -jnp.inf), axis=-1)
        return jnp.einsum('bhqk,bkhd->bqhd', p.astype(v.dtype), v)

    out = lax.map(attend, (q_blocks, jnp.arange(nb)))
    return out.transpose(1, 0, 2, 3, 4).reshape(b, s, h * dv)

def setup_inputs(seed: int = 0) -> dict:
    key = jax.random.key(seed)
    ks = jax.random.split(key, 20)

    def nrm(k, shape, fan_in):
        return jax.random.normal(k, shape, jnp.float32) * fan_in ** -0.5

    def gain(k, n):
        return 1.0 + 0.02 * jax.random.normal(k, (DEPTH, n), jnp.float32)

    x = jax.random.normal(ks[0], (BATCH, SEQ, D_MODEL), jnp.float32)
    offsets = jax.random.randint(ks[1], (BATCH, 1), 0, MAX_STREAM_OFFSET, dtype=jnp.int32)
    positions = offsets + jnp.arange(SEQ, dtype=jnp.int32)[None, :]
    w_in = nrm(ks[2], (DEPTH, D_MODEL, PROJ_WIDTH), D_MODEL)
    conv_w = nrm(ks[3], (DEPTH, CONV_WIDTH, GDN_QKV), CONV_WIDTH)
    A_log = jnp.log(jax.random.uniform(ks[4], (DEPTH, GDN_HEADS), jnp.float32, 1.0, 16.0))
    dt = jnp.exp(jax.random.uniform(ks[5], (DEPTH, GDN_HEADS), jnp.float32, math.log(1e-3), math.log(1e-1)))
    dt_bias = dt + jnp.log(-jnp.expm1(-dt))
    gdn_norm_w = gain(ks[6], GDN_DV)
    q_a_norm_w = gain(ks[7], MLA_Q_LORA)
    w_uq = nrm(ks[8], (DEPTH, MLA_Q_LORA, MLA_HEADS * MLA_QK_DIM), MLA_Q_LORA)
    kv_a_norm_w = gain(ks[9], MLA_KV_LORA)
    w_ukv = nrm(ks[10], (DEPTH, MLA_KV_LORA, MLA_HEADS * (MLA_NOPE + MLA_V)), MLA_KV_LORA)
    w_branch_a = nrm(ks[11], (DEPTH, GDN_HEADS * GDN_DV, D_MODEL), GDN_HEADS * GDN_DV)
    w_branch_b = nrm(ks[12], (DEPTH, MLA_HEADS * MLA_V, D_MODEL), MLA_HEADS * MLA_V)
    w_out = nrm(ks[13], (DEPTH, D_MODEL, D_MODEL), D_MODEL)
    pre_mix_norm_w = gain(ks[14], D_MODEL)
    post_mix_norm_w = gain(ks[15], D_MODEL)
    pre_ffn_norm_w = gain(ks[16], D_MODEL)
    post_ffn_norm_w = gain(ks[17], D_MODEL)
    w_ff1 = nrm(ks[18], (DEPTH, D_MODEL, D_FF), D_MODEL)
    w_ff2 = nrm(ks[19], (DEPTH, D_FF, D_MODEL), D_FF)
    return {"x": x, "positions": positions, "w_in": w_in, "conv_w": conv_w, "A_log": A_log,
            "dt_bias": dt_bias, "gdn_norm_w": gdn_norm_w, "q_a_norm_w": q_a_norm_w, "w_uq": w_uq,
            "kv_a_norm_w": kv_a_norm_w, "w_ukv": w_ukv, "w_branch_a": w_branch_a, "w_branch_b": w_branch_b,
            "w_out": w_out, "pre_mix_norm_w": pre_mix_norm_w, "post_mix_norm_w": post_mix_norm_w,
            "pre_ffn_norm_w": pre_ffn_norm_w, "post_ffn_norm_w": post_ffn_norm_w, "w_ff1": w_ff1, "w_ff2": w_ff2}

def reference(x, positions, w_in, conv_w, A_log, dt_bias, gdn_norm_w, q_a_norm_w, w_uq, kv_a_norm_w, w_ukv,
              w_branch_a, w_branch_b, w_out, pre_mix_norm_w, post_mix_norm_w, pre_ffn_norm_w, post_ffn_norm_w,
              w_ff1, w_ff2):
    b, s, _ = x.shape
    inv_freq = ROPE_BASE ** (-jnp.arange(0, MLA_ROPE, 2, dtype=jnp.float32) / MLA_ROPE)
    ang = positions.astype(jnp.float32)[..., None] * inv_freq
    cos, sin = jnp.cos(ang).astype(x.dtype), jnp.sin(ang).astype(x.dtype)

    for l in range(DEPTH):
        u = _rms_norm(x, pre_mix_norm_w[l])
        proj = u @ w_in[l]
        qkv_a, z_a, a_a, b_a, cq, ckv, k_rope, gate_logits = _split_cols(proj, PROJ_SIZES)

        qkv_a = jax.nn.silu(_causal_conv(qkv_a, conv_w[l]))
        q_a, k_a, v_a = _split_cols(qkv_a, (GDN_HEADS * GDN_DK, GDN_HEADS * GDN_DK, GDN_HEADS * GDN_DV))
        q_a = _l2_norm(q_a.reshape(b, s, GDN_HEADS, GDN_DK).astype(jnp.float32))
        k_a = _l2_norm(k_a.reshape(b, s, GDN_HEADS, GDN_DK).astype(jnp.float32))
        v_a = v_a.reshape(b, s, GDN_HEADS, GDN_DV)
        g_a = -jnp.exp(A_log[l].astype(jnp.float32)) * jax.nn.softplus(
            a_a.astype(jnp.float32) + dt_bias[l].astype(jnp.float32))
        beta_a = jax.nn.sigmoid(b_a.astype(jnp.float32))
        o_a = _gated_delta_rule(q_a, k_a, v_a, g_a, beta_a)
        o_a = _rms_norm(o_a, gdn_norm_w[l]) * jax.nn.silu(z_a.reshape(b, s, GDN_HEADS, GDN_DV))
        y_a = o_a.reshape(b, s, GDN_HEADS * GDN_DV) @ w_branch_a[l]

        q_b = (_rms_norm(cq, q_a_norm_w[l]) @ w_uq[l]).reshape(b, s, MLA_HEADS, MLA_QK_DIM)
        q_b = jnp.concatenate([q_b[..., :MLA_NOPE], _rope(q_b[..., MLA_NOPE:], cos[:, :, None, :], sin[:, :, None, :])], axis=-1)
        kv_b = (_rms_norm(ckv, kv_a_norm_w[l]) @ w_ukv[l]).reshape(b, s, MLA_HEADS, MLA_NOPE + MLA_V)
        k_nope, v_b = kv_b[..., :MLA_NOPE], kv_b[..., MLA_NOPE:]
        k_pe = jnp.broadcast_to(_rope(k_rope, cos, sin)[:, :, None, :], (b, s, MLA_HEADS, MLA_ROPE))
        k_b = jnp.concatenate([k_nope, k_pe], axis=-1)
        y_b = _chunk_causal_attention(q_b, k_b, v_b) @ w_branch_b[l]

        gates = jax.nn.sigmoid(gate_logits.reshape(b, s, N_BRANCHES, D_MODEL))
        h = gates[:, :, 0] * y_a + gates[:, :, 1] * y_b
        x = x + _rms_norm(h @ w_out[l], post_mix_norm_w[l])

        u = _rms_norm(x, pre_ffn_norm_w[l])
        f = jnp.square(jax.nn.relu(u @ w_ff1[l])) @ w_ff2[l]
        x = x + _rms_norm(f, post_ffn_norm_w[l])
    return x


_drawn_inputs = setup_inputs


def setup_inputs(seed=0):
    import zlib

    import numpy as np

    out = dict(_drawn_inputs(seed))
    spreads = {}
    factors = {'gdn_norm_w': 15.228,
     'q_a_norm_w': 8.0,
     'kv_a_norm_w': 6.715,
     'pre_ffn_norm_w': 2.968,
     'post_ffn_norm_w': 3.231}
    for name, (base, spread) in spreads.items():
        noise = np.random.default_rng([zlib.crc32(name.encode()), seed]).standard_normal(out[name].shape)
        drawn = base * np.exp(spread * noise) if base else spread * noise
        out[name] = jnp.asarray(drawn.astype(out[name].dtype))
    for name, factor in factors.items():
        out[name] = (out[name] * factor).astype(out[name].dtype)
    return out
```

```python
from contextlib import ExitStack
import math

import numpy as np
import concourse.bass as bass
from concourse import mybir

F32 = mybir.dt.float32
F32R = mybir.dt.float32r
I32 = mybir.dt.int32
ALU = mybir.AluOpType
ACT = mybir.ActivationFunctionType
AX = mybir.AxisListType.X

P = 128
DEPTH, D, S = 2, 1024, 256
KD = D // P
NT = S // P
H, DK = 8, 128
ROPE, QL, KVL = 64, 384, 256
KQ, KKV = QL // P, KVL // P
EPS = 1e-6
CHUNK = 64
QKV = 3 * H * DK
FF = 4 * D
KF = FF // P
PIECE = 1024
PI_BELOW = 3.1415925
RING = 4
SIZES = [2 ** i for i in range(1, 7)]

PRE_MIX, POST_MIX, PRE_FFN, POST_FFN, CONV = 0, KD, 2 * KD, 3 * KD, 4 * KD
QA = CONV + 4 * (QKV // P)
KVA = QA + KQ
GDN = KVA + KKV
ALOG = GDN + 1
DTB = ALOG + H
NPRM = DTB + H

C_ID, C_UT, C_NEG, C_M1, C_LV, C_ONE, C_PERM, C_AM, C_FREQ = 0, 128, 256, 384, 512, 896, 1024, 1152, 1408
NCST = C_FREQ + 4


def jobs_of_a_layer():
    jobs, n = [], 0
    for kind, count, pieces in (("v", 4, 2), ("q", 4, 2), ("k", 4, 2), ("lat", 3, 2), ("uq", 6, 1), ("kn", 4, 0.5),
                                ("vt", 4, 0.5), ("z", 4, 2), ("gate", 8, 2), ("ya", 4, 2), ("yb", 4, 2),
                                ("out", 4, 2), ("ff1", 16, 2), ("ff2", 4, 8)):
        for i in range(count):
            jobs.append((kind, i, list(range(int(n), max(int(n) + 1, int(n + pieces))))))
            n += pieces
    return jobs, int(n)


JOBS, NPIECE = jobs_of_a_layer()
FIRST = {}
for _j, (_k, _i, _p) in enumerate(JOBS):
    FIRST.setdefault(_k, _j)
EVAC_BY_ACT = {"v", "q", "k", "lat", "uq", "kn", "vt", "z"}
NJOB = len(JOBS)
NACT_EVAC = sum(k in EVAC_BY_ACT for k, _, _ in JOBS)
NDVE_EVAC = NJOB - NACT_EVAC




def steps_through(n, job=False):
    if job:
        return sum(len(p) for _, _, p in JOBS[:n + 1])
    if n < 0:
        return n + 1
    return sum(len([q for q in p if q <= n]) for _, _, p in JOBS)


NSTEP = steps_through(NJOB - 1, job=True)


def evacs_through(j):
    mine = JOBS[j][0] in EVAC_BY_ACT
    return mine, sum((k in EVAC_BY_ACT) == mine for k, _, _ in JOBS[:j + 1])


def schedule():
    o = [("start", 0), ("pre", 0)]
    late = []

    def job(kind, i, after=None):
        o.append(("job", FIRST[kind] + i))
        flush()
        if after:
            late.append((after, i))

    def flush():
        o.extend(late)
        late.clear()

    for i in range(4):
        job("v", i)
        if i == 0:
            o.append(("ab", 0))
        o.append(("conv", i))
        if i == 1:
            o += [("logits", 0), ("silu", 0)]
        if i:
            late.append(("silu", i))
        if i == 2:
            o.append(("gc", 0))
    for i in range(4):
        job("q", i)
        o.append(("conv", 4 + i))
        late.append(("silu", 4 + i))
        o += [("vtrans", i), ("dt", i)]
    for i in range(4):
        job("k", i)
        o.append(("conv", 8 + i))
        late.append(("silu", 8 + i))
    flush()
    o.append(("lnexp", 0))
    for i in range(8):
        o.append(("nrm", i))
        flush()
        if i in (1, 3, 5):
            job("lat", i // 2)
            late.append(("latn", i // 2))
    fill = [("uq", i) for i in range(6)] + [("kn", i) for i in range(4)] + [("vt", i) for i in range(4)]
    o += [("ktrans", 0), ("ktrans", 1)]
    for g in range(4):
        o.append(("decay", g))
        job(*fill.pop(0)) if g < 2 else None
    for g in range(4):
        o.append(("x1", g))
    for lv in range(len(SIZES)):
        for step in ("lvP", "lvV", "lvT"):
            for g in range(4):
                o.append((step, lv * 4 + g))
            if fill and step != "lvT":
                kind, i = fill.pop(0)
                job(kind, i)
                if kind == "uq" and i >= 4:
                    late.append(("qrope", i - 4))
    flush()
    assert not fill
    steps = ("t_v0", "t_st", "t_ks", "t_v1", "t_o")
    for n, step in enumerate(steps):
        o += [(step, 0), (step, 1)]
        if n < 4:
            job("z", n)
    o.append(("lnexp", 1))
    for i in range(4):
        o.append(("onrm", i))
        if i % 2:
            job("gate", i // 2)
        if i:
            o.append(("osplit", i - 1))
    o += [("osplit", 3), ("sc", 0), ("sc", 1)]
    for n in range(6):
        job("gate", 2 + n)
        o.append(("tr", n))
        if n + 2 < 6:
            o.append(("sc", n + 2))
        o.append(("pv", n))
    o.append(("sig", 0))
    for i in range(4):
        job("ya", i)
    for i in range(4):
        job("yb", i, "hsplit")
    flush()
    for i in range(4):
        job("out", i)
        late.append(("ysum", i))
    flush()
    o += [("post", 0), ("pre", 1)]
    for i in range(16):
        job("ff1", i, "fsplit")
    flush()
    for i in range(4):
        job("ff2", i)
        late.append(("ysum", 4 + i))
    flush()
    o.append(("post", 1))
    return o


ORDER = schedule()


def build(nc, x_in, pos_in, w_in, ab_in, prm_in, cst_in, out):
    with ExitStack() as ctx:
        base = [((nc.sbuf_base + 31) // 32) * 32]

        def at(name, shape, dtype, offset):
            return nc.alloc_sbuf_tensor_at(name, shape, dtype, offset=offset)

        def size(shape):
            return int(np.prod(shape[1:])) * 4

        def keep(name, shape, dtype=F32):
            t = at(name, shape, dtype, base[0])
            base[0] += (size(shape) + 31) // 32 * 32
            return t

        def psum(name):
            return ctx.enter_context(nc.psum_tensor(name, [P, 512], F32))

        xT = keep("xT", [P, KD, S])
        raw = [keep(f"raw{i}", [P, PIECE]) for i in range(RING)]
        whi = [keep(f"whi{i}", [P, PIECE], F32R) for i in range(RING)]
        wlo = [keep(f"wlo{i}", [P, PIECE], F32R) for i in range(RING)]
        cst = keep("cst", [P, NCST])
        prm_all = keep("prm_all", [P, DEPTH, NPRM])
        prm = keep("prm", [P, NPRM])
        cosT = keep("cosT", [P, S])
        sinT = keep("sinT", [P, S])
        sq = [keep(f"sq{i}", [P, 512]) for i in range(2)]
        rn = [keep(f"rn{i}", [P, 512]) for i in range(2)]
        ab_all = keep("ab_all", [P, DEPTH, KD * 16])
        ab_hi = keep("ab_hi", [P, KD * 16], F32R)
        ab_lo = keep("ab_lo", [P, KD * 16], F32R)
        sm = keep("sm", [P, 14, 32])
        gcT = keep("gcT", [8, S])
        mx = keep("mx", [P, 4])
        rs = keep("rs", [P, 4])
        bias_cols = keep("bias_cols", [P, 2])
        eps_col, lnscale_col = bias_cols[:, 0:1], bias_cols[:, 1:2]

        R0 = base[0]
        KIB = 1024

        def ph(name, shape, kib, dtype=F32):
            assert R0 + kib * KIB + size(shape) <= nc.sbuf_usable_end, name
            return at(name, shape, dtype, R0 + int(kib * KIB))

        uh = ph("uh", [P, KD, S], 0, F32R)
        ul = ph("ul", [P, KD, S], 8, F32R)
        qT = ph("qT", [P, H, S], 16)
        kT = ph("kT", [P, H, S], 24)
        vT = ph("vT", [P, H, S], 32)
        vtok = ph("vtok", [P, NT, H, DK], 40)
        ktok = ph("ktok", [P, H, DK], 48)
        DT = ph("DT", [P, 4, 4, P], 52)
        LT = ph("LT", [P, 4, 4, P], 60)
        XT = ph("XT", [P, 4, 4, P], 68)
        AT = ph("AT", [P, 4, 4, P], 76)
        cb = [ph(f"cb{i}", [P, 2, S], 99 + 2 * i) for i in range(2)]
        sq_kv = ph("sq_kv", [P, 2 * S], 76)
        sq_q = ph("sq_q", [P, 3 * S], 78)
        krx = ph("krx", [P, S], 81)
        kra = ph("kra", [P, S], 82)
        rl = ph("rl", [P, S], 83)
        latT = ph("latT", [P, 5, S], 84)
        lath = ph("lath", [P, 5, S], 89, F32R)
        latl = ph("latl", [P, 5, S], 94, F32R)
        qn = ph("qn", [P, H, S], 99)
        qr = ph("qr", [P, 4, S], 107)
        kn = ph("kn", [P, H, S], 111)
        kr = ph("kr", [P, S], 119)
        krz = ph("krz", [P, 2, S], 84)
        vt = ph("vt", [P, NT, H, DK], 120)
        utmp = ph("utmp", [P, KD, S], 99)
        usq = ph("usq", [P, KD, S], 107)
        abT = ph("abT", [16, S], 116)
        X = ph("X", [P, 4, 4, P], 52)
        PB = ph("PB", [P, 4, 4, 64], 32)
        qd = ph("qd", [P, H, P], 36)
        zs = ph("zs", [P, H, S], 16)
        vn0 = ph("vn0", [P, H, DK], 52)
        st = ph("st", [P, H, DK], 56)
        vn1 = ph("vn1", [P, H, DK], 60)
        rr = ph("rr", [P, H, DK], 64)
        oT = ph("oT", [P, H, S], 24)
        oh = ph("oh", [P, H, S], 91, F32R)
        ol = ph("ol", [P, H, S], 32, F32R)
        gates = ph("gates", [P, 2, KD, S], 40)
        E = [ph(f"E{i}", [P, 512], 60 + 2 * i) for i in range(2)]
        PT = [ph(f"PT{i}", [P, 512], 64 + 2 * i) for i in range(2)]
        ah = ph("ah", [P, H, S], 68, F32R)
        al = ph("al", [P, H, S], 76, F32R)
        hA = ph("hA", [P, KD, S], 16)
        hB = [ph(f"hB{i}", [P, 512], 24 + 2 * i) for i in range(2)]
        hh = ph("hh", [P, KD, S], 99, F32R)
        hl = ph("hl", [P, KD, S], 111, F32R)
        fuh = ph("fuh", [P, KD, S], 0, F32R)
        ful = ph("ful", [P, KD, S], 8, F32R)
        yT = ph("yT", [P, KD, S], 120)
        futmp = ph("futmp", [P, KD, S], 16)
        fusq = ph("fusq", [P, KD, S], 24)
        fh = ph("fh", [P, KF, S], 16, F32R)
        fl = ph("fl", [P, KF, S], 48, F32R)
        fr = [ph(f"fr{i}", [P, 512], 80 + 2 * i) for i in range(4)]
        pos_i = ph("pos_i", [P, S], 0, I32)
        ang = ph("ang", [P, 4, S], 8)

        dense = [psum(f"dense{i}") for i in range(3)]
        side = [psum(f"side{i}") for i in range(5)]

        ident = cst[:, C_ID:C_ID + P]
        upto = cst[:, C_UT:C_UT + P]
        future = cst[:, C_NEG:C_NEG + P]
        below1 = cst[:, C_M1:C_M1 + P]
        ones = cst[:, C_ONE:C_ONE + P]
        perm = cst[:, C_PERM:C_PERM + P]
        amask = cst[:, C_AM:C_AM + S]

        def over_heads(ap, n):
            return ap.rearrange("p (a w) -> p a w", a=1).broadcast_to([P, n, ap.shape[1]])

        def along(ap, w):
            return ap.rearrange("p (n a) -> p n a", a=1).broadcast_to([P, ap.shape[1], w])

        def S_(name):
            return ctx.enter_context(nc.semaphore(name))

        loaded = [S_(f"loaded{i}") for i in range(RING)]
        s_in, s_out = S_("s_in"), S_("s_out")
        s_trig, s_trig_a = S_("s_trig"), S_("s_trig_a")
        hi_ready, lo_ready, steps_done = S_("hi_ready"), S_("lo_ready"), S_("steps_done")
        act_evac, dve_evac = S_("act_evac"), S_("dve_evac")
        rises_per_layer = {}

        def signal(name, rises):
            s = S_(name)
            rises_per_layer[s.name] = rises
            return s

        weighted, x_by_pool, x_by_dve = (signal("weighted", 2), signal("x_by_pool", 4), signal("x_by_dve", 4))
        prm_ready, squared, sumsq, rnorm = (signal("prm_ready", 1), signal("squared", 8), signal("sumsq", 2), signal("rnorm", 4))
        pre_scaled, u_hi, u_lo, ab_split_hi = (signal("pre_scaled", 8), signal("u_hi", 8), signal("u_lo", 8), signal("ab_split_hi", 1))
        ab_t, ab_t_copied = (signal("ab_t", 1), signal("ab_t_copied", 1))
        ab_split_lo, ab_mm, ab_z, ab_abs = (signal("ab_split_lo", 1), signal("ab_mm", 1), signal("ab_z", 2), signal("ab_abs", 1))
        ab_ex, ab_w, ab_ln, ab_rc = (signal("ab_ex", 1), signal("ab_w", 2), signal("ab_ln", 1), signal("ab_rc", 1))
        ab_sp, ab_a, ab_g, gc_mm = (signal("ab_sp", 3), signal("ab_a", 2), signal("ab_g", 1), signal("gc_mm", 1))
        gc_copied, gc_exp, conv_mid, silu_done = (signal("gc_copied", 3), signal("gc_exp", 2), signal("conv_mid", 72), signal("silu_done", 12))
        tap0, dt_fut, dt_mm, dt_arg = (signal("tap0", 12), signal("dt_fut", 4), signal("dt_mm", 4), signal("dt_arg", 4))
        vtrans_mm, vtrans_out, nrm_sq, nrm_mm = (signal("vtrans_mm", 4), signal("vtrans_out", 4), signal("nrm_sq", 8), signal("nrm_mm", 8))
        nrm_r, nrm_out, lat_sq, lat_mm = (signal("nrm_r", 16), signal("nrm_out", 8), signal("lat_sq", 3), signal("lat_mm", 2))
        lat_r, lat_norm, lat_hi, lat_lo = (signal("lat_r", 4), signal("lat_norm", 5), signal("lat_hi", 2), signal("lat_lo", 2))
        kr_mm, kr_b, kr_out, ktrans_mm = (signal("kr_mm", 1), signal("kr_b", 3), signal("kr_out", 2), signal("ktrans_mm", 2))
        ktrans_out, dec_mm, dec_exp = (signal("ktrans_out", 2), signal("dec_mm", 4), signal("dec_exp", 4))
        dec_eg, dec_out, qd_out = (signal("dec_eg", 2), signal("dec_out", 8), signal("qd_out", 2))
        x1_mask, x1_xt, x1_mm, x1_out = (signal("x1_mask", 4), signal("x1_xt", 4), signal("x1_mm", 4), signal("x1_out", 4))
        lv_p, lv_p_out, lv_v = (signal("lv_p", 24), signal("lv_p_out", 24), signal("lv_v", 24))
        lv_x, lv_t, lv_t_out = (signal("lv_x", 24), signal("lv_t", 24), signal("lv_t_out", 24))
        t_v0m, t_v0o, t_stm, t_sto = (signal("t_v0m", 2), signal("t_v0o", 2), signal("t_stm", 2), signal("t_sto", 2))
        t_ksm, t_kst, t_kso, t_v1m = (signal("t_ksm", 2), signal("t_kst", 2), signal("t_kso", 2), signal("t_v1m", 2))
        t_v1o, t_om, t_oo, on_sq = (signal("t_v1o", 2), signal("t_om", 2), signal("t_oo", 2), signal("on_sq", 4))
        on_mm, on_r, on_o, on_z = (signal("on_mm", 4), signal("on_r", 8), signal("on_o", 4), signal("on_z", 4))
        on_hi, on_lo, qr_mm, qr_b = (signal("on_hi", 4), signal("on_lo", 4), signal("qr_mm", 2), signal("qr_b", 4))
        qr_out, sc_mm, sm_mask, sm_max = (signal("qr_out", 2), signal("sc_mm", 6), signal("sm_mask", 6), signal("sm_max", 6))
        sm_sub, sm_exp, sm_sum, sm_rec = (signal("sm_sub", 6), signal("sm_exp", 6), signal("sm_sum", 6), signal("sm_rec", 6))
        sm_out, tr_mm, tr_out, pv_mm = (signal("sm_out", 6), signal("tr_mm", 6), signal("tr_out", 6), signal("pv_mm", 6))
        pv_hi, pv_lo, sig_done, h_sum = (signal("pv_hi", 6), signal("pv_lo", 6), signal("sig_done", 4), signal("h_sum", 4))
        h_hi, h_lo, y_sq, y_mm = (signal("h_hi", 4), signal("h_lo", 4), signal("y_sq", 8), signal("y_mm", 8))
        y_r, y_scaled, f_sq = (signal("y_r", 4), signal("y_scaled", 8), signal("f_sq", 16))
        f_hi, f_lo = (signal("f_hi", 16), signal("f_lo", 16))

        block = ctx.enter_context(nc.Block())

        def due(l, s, n):
            return l * rises_per_layer[s.name] + n

        def products_done(l, j):
            return l * NSTEP + steps_through(j, job=True) + RING

        def unit(n):
            return (0, range(4 * n, 4 * n + 4)) if n < 2 else (1, range(2 * (n - 2), 2 * (n - 2) + 2))

        def conv_place(n):
            return [vT, qT, kT][n // 4], [2 * H, 0, H][n // 4] + 2 * (n % 4)

        def heads_of(g):
            return range(4 * (g % 2), 4 * (g % 2) + 4)

        def piece_width(n):
            kind = next(k for k, _, p in JOBS if n in p)
            return KQ * 256 if kind == "uq" else PIECE

        def splits_wanted(j):
            return min(JOBS[j][2][-1] + RING + (JOBS[j][0] not in ("uq", "kn", "vt")), NPIECE)

        splits_at, seen = [], 0
        for what, n in ORDER:
            goal = RING if what == "start" else splits_wanted(n) if what == "job" else seen
            splits_at.append(range(seen, max(seen, goal)))
            seen = max(seen, goal)
        assert seen == NPIECE

        @block.sync
        def _(sp):
            sp.dma_start(xT[:], x_in).then_inc(s_in, 16)
            sp.dma_start(pos_i[:], pos_in).then_inc(s_in, 16)
            sp.dma_start(cst[:], cst_in).then_inc(s_in, 16)
            sp.dma_start(prm_all[:], prm_in).then_inc(s_in, 16)
            sp.dma_start(ab_all[:], ab_in).then_inc(s_in, 16)
            with sp.Fori(0, DEPTH * NPIECE // RING) as i:
                for s in range(RING):
                    sp.wait_ge(lo_ready, i * RING + s + 1)
                    sp.dma_start(raw[s][:], w_in[i * RING + s]).then_inc(loaded[s], 16)
            sp.wait_ge(x_by_pool, due(DEPTH, x_by_pool, 2))
            sp.wait_ge(x_by_dve, due(DEPTH, x_by_dve, 2))
            sp.dma_start(out, xT[:]).then_inc(s_out, 16)
            sp.wait_ge(s_out, 16)

        @block.tensor
        def _(pe):
            mm = nc.tensor.matmul
            pe.sem_inc(steps_done, RING)

            def banks_free(l, j):
                if j >= 3:
                    by_act, n = evacs_through(j - 3)
                    if by_act:
                        pe.wait_ge(act_evac, l * NACT_EVAC + n)
                    else:
                        pe.wait_ge(dve_evac, l * NDVE_EVAC + n)

            def piece(l, n):
                pe.wait_ge(lo_ready, l * NPIECE + n + 1 + RING)
                return whi[n % RING], wlo[n % RING]

            def chunk_products(bank, n, k0, kcount, cols, ahi, alo, first, last, total_k, need=None):
                h_, l_ = whi[n % RING], wlo[n % RING]
                nch = cols // P
                for k in range(kcount):
                    if need is not None:
                        need(k0 + k)
                    for c in range(nch):
                        ws = slice(k * cols + c * P, k * cols + (c + 1) * P)
                        o_ = bank[:, c * S:(c + 1) * S]
                        is_first = first and k == 0 and c == 0
                        is_last = last and k == kcount - 1 and c == nch - 1
                        mm(o_, h_[:, ws], ahi[:, k0 + k, :], start=is_first, stop=False, skip_group_check=True)
                        mm(o_, h_[:, ws], alo[:, k0 + k, :], start=False, stop=False, skip_group_check=True)
                        x_ = mm(o_, l_[:, ws], ahi[:, k0 + k, :], start=False, stop=is_last, skip_group_check=True)
                return x_

            def job(l, j):
                kind, i, pieces = JOBS[j]
                bank = dense[j % 3]
                banks_free(l, j)
                if kind in ("v", "q", "k", "z", "gate", "lat"):
                    def need(k):
                        if kind == "v" and i == 0:
                            pe.wait_ge(u_lo, due(l, u_lo, k // 2 + 1))
                    for h_, n in enumerate(pieces):
                        piece(l, n)
                        r = chunk_products(bank, n, 4 * h_, 4, 256, uh, ul, h_ == 0, h_ == 1, KD, need)
                        r.then_inc(steps_done, 1)
                elif kind in ("ya", "yb", "out"):
                    a_, b_ = {"ya": (oh, ol), "yb": (ah, al), "out": (hh, hl)}[kind]
                    if kind == "yb" and i == 0:
                        pe.wait_ge(pv_lo, due(l, pv_lo, 6))

                    def need(k):
                        if kind == "ya" and i == 0:
                            pe.wait_ge(on_lo, due(l, on_lo, k // 2 + 1))
                        if kind == "out" and i == 0:
                            pe.wait_ge(h_lo, due(l, h_lo, k // 2 + 1))
                    for h_, n in enumerate(pieces):
                        piece(l, n)
                        r = chunk_products(bank, n, 4 * h_, 4, 256, a_, b_, h_ == 0, h_ == 1, KD, need)
                        r.then_inc(steps_done, 1)
                elif kind == "uq":
                    n = pieces[0]
                    piece(l, n)
                    if i == 0:
                        pe.wait_ge(lat_lo, due(l, lat_lo, 2))
                    r = chunk_products(bank, n, KKV, KQ, 256, lath, latl, True, True, KQ)
                    r.then_inc(steps_done, 1)
                elif kind == "kn":
                    n = pieces[0]
                    piece(l, n)
                    for c in range(2):
                        for k in range(KKV):
                            ws = slice(k * 512 + ((i % 2) * 2 + c) * P, k * 512 + ((i % 2) * 2 + c + 1) * P)
                            o_ = bank[:, c * S:(c + 1) * S]
                            mm(o_, whi[n % RING][:, ws], lath[:, k, :], start=(k == 0), stop=False)
                            mm(o_, whi[n % RING][:, ws], latl[:, k, :], start=False, stop=False)
                            r = mm(o_, wlo[n % RING][:, ws], lath[:, k, :], start=False, stop=(k == KKV - 1))
                    r.then_inc(steps_done, 1)
                elif kind == "vt":
                    n = pieces[0]
                    piece(l, n)
                    t = i % 2
                    for k in range(KKV):
                        a_, b_ = lath[:, k, t * P:(t + 1) * P], latl[:, k, t * P:(t + 1) * P]
                        ws = slice(k * 512, (k + 1) * 512)
                        mm(bank[:], a_, whi[n % RING][:, ws], start=(k == 0), stop=False)
                        mm(bank[:], a_, wlo[n % RING][:, ws], start=False, stop=False)
                        r = mm(bank[:], b_, whi[n % RING][:, ws], start=False, stop=(k == KKV - 1))
                    r.then_inc(steps_done, 1)
                elif kind == "ff1":
                    def need1(k):
                        if i == 0:
                            pe.wait_ge(u_lo, due(l, u_lo, 4 + k // 2 + 1))
                    for h_, n in enumerate(pieces):
                        piece(l, n)
                        r = chunk_products(bank, n, 4 * h_, 4, 256, fuh, ful, h_ == 0, h_ == 1, KD, need1)
                        r.then_inc(steps_done, 1)
                elif kind == "ff2":
                    for h_, n in enumerate(pieces):
                        piece(l, n)
                        if i == 0:
                            pe.wait_ge(f_lo, due(l, f_lo, 2 * h_ + 2))
                        r = chunk_products(bank, n, 4 * h_, 4, 256, fh, fl, h_ == 0, h_ == 7, KF)
                        r.then_inc(steps_done, 1)

            def pre(l, w):
                q_ = fusq if w else usq
                for c in range(KD):
                    if c % 2 == 0:
                        pe.wait_ge(squared, due(l, squared, 4 * w + c // 2 + 1))
                    r = mm(side[0][:, 0:S], ones, q_[:, c, :], start=(c == 0), stop=(c == KD - 1))
                r.then_inc(sumsq, 1)

            def ab(l, _):
                pe.wait_ge(ab_split_lo, due(l, ab_split_lo, 1))
                pe.wait_ge(u_lo, due(l, u_lo, 4))
                for k in range(KD):
                    ws = slice(16 * k, 16 * k + 16)
                    o_ = side[1][0:16, 0:S]
                    mm(o_, ab_hi[:, ws], uh[:, k, :], start=(k == 0), stop=False)
                    mm(o_, ab_hi[:, ws], ul[:, k, :], start=False, stop=False)
                    r = mm(o_, ab_lo[:, ws], uh[:, k, :], start=False, stop=(k == KD - 1))
                r.then_inc(ab_t, 1)

            def logits(l, _):
                pe.wait_ge(ab_t_copied, due(l, ab_t_copied, 1))
                for t in range(NT):
                    r = mm(side[2][:, 16 * t:16 * t + 16], abT[:, t * P:(t + 1) * P], cst[0:16, C_ID:C_ID + 16],
                           start=True, stop=True)
                r.then_inc(ab_mm, 1)

            def gc(l, _):
                g_ = sm[:, 8, :].rearrange("p (t n) -> p t n", t=NT)
                pe.wait_ge(ab_g, due(l, ab_g, 1))
                pe.wait_ge(ab_a, due(l, ab_a, 2))
                mm(side[2][:, 0:32], upto, sm[:, 8, :], start=True, stop=True)
                mm(side[2][:, 32:64], ones, sm[:, 8, :], start=True, stop=True)
                for t in range(NT):
                    r = mm(side[2][0:8, 128 + t * P:128 + (t + 1) * P], g_[:, t, 0:8], upto, start=True, stop=True)
                r.then_inc(gc_mm, 1)

            def dt(l, g):
                pe.wait_ge(gc_copied, due(l, gc_copied, 3))
                if g == 3:
                    pe.wait_ge(dt_arg, due(l, dt_arg, 1))
                t = g // 2
                for e, h in enumerate(heads_of(g)):
                    one_row = cst[0:8, C_ID + h:C_ID + h + 1].broadcast_to([8, P])
                    r = mm(side[g % 3][:, e * P:(e + 1) * P], one_row, gcT[:, t * P:(t + 1) * P], start=True, stop=True)
                r.then_inc(dt_mm, 1)

            def vtrans(l, i):
                t, half = i // 2, i % 2
                if i == 0:
                    pe.wait_ge(silu_done, due(l, silu_done, 4))
                if i >= 2:
                    pe.wait_ge(vtrans_out, due(l, vtrans_out, i - 1))
                for e in range(4):
                    r = nc.tensor.transpose(side[3 + i % 2][:, e * P:(e + 1) * P],
                                            vT[:, 4 * half + e, t * P:(t + 1) * P], ident)
                r.then_inc(vtrans_mm, 1)

            def nrm(l, i):
                pe.wait_ge(nrm_sq, due(l, nrm_sq, i + 1))
                if i == 0:
                    pe.wait_ge(dt_arg, due(l, dt_arg, 2))
                    pe.wait_ge(vtrans_out, due(l, vtrans_out, 3))
                if i >= 2:
                    pe.wait_ge(nrm_r, due(l, nrm_r, 2 * (i - 2) + 1))
                mm(side[1 + 2 * (i % 2)][:], ones, sq[i % 2][:], start=True, stop=True).then_inc(nrm_mm, 1)

            def latn(l, i):
                if i == 0:
                    pe.wait_ge(vtrans_out, due(l, vtrans_out, 4))
                    pe.wait_ge(lat_sq, due(l, lat_sq, 1))
                    for e in range(2):
                        r = mm(side[4][:, 0:S], ones, sq_kv[:, e * S:(e + 1) * S], start=(e == 0), stop=(e == 1))
                    r.then_inc(lat_mm, 1)
                elif i == 2:
                    pe.wait_ge(lat_r, due(l, lat_r, 1))
                    pe.wait_ge(act_evac, l * NACT_EVAC + evacs_through(FIRST["lat"] + 2)[1])
                    mm(side[4][:, S:2 * S], perm, krx[:], start=True, stop=True).then_inc(kr_mm, 1)
                    pe.wait_ge(lat_sq, due(l, lat_sq, 3))
                    for e in range(3):
                        r = mm(side[4][:, 0:S], ones, sq_q[:, e * S:(e + 1) * S], start=(e == 0), stop=(e == 2))
                    r.then_inc(lat_mm, 1)

            def ktrans(l, half):
                pe.wait_ge(nrm_out, due(l, nrm_out, 6 + 2 * half))
                if half == 0:
                    pe.wait_ge(dec_eg, due(l, dec_eg, 1))
                for e in range(4):
                    r = nc.tensor.transpose(side[2 + half][:, e * P:(e + 1) * P], kT[:, 4 * half + e, 0:P], ident)
                r.then_inc(ktrans_mm, 1)

            def decay(l, g):
                b_ = 2 * (g % 2)
                if g == 0:
                    pe.wait_ge(nrm_out, due(l, nrm_out, 8))
                    pe.wait_ge(dec_eg, due(l, dec_eg, 2))
                elif g == 1:
                    pe.wait_ge(ktrans_out, due(l, ktrans_out, 2))
                else:
                    pe.wait_ge(dec_out, due(l, dec_out, 2 * (g - 1)))
                for e, h in enumerate(heads_of(g)):
                    cols = slice(e * P, (e + 1) * P)
                    ts_ = slice(g // 2 * P, (g // 2 + 1) * P)
                    mm(side[b_][:, cols], kT[:, h, ts_], kT[:, h, ts_], start=True, stop=True)
                    r = mm(side[b_ + 1][:, cols], kT[:, h, ts_], qT[:, h, ts_], start=True, stop=True)
                r.then_inc(dec_mm, 1)

            def x1(l, g):
                pe.wait_ge(x1_xt, due(l, x1_xt, g + 1))
                pe.wait_ge(dec_out, due(l, dec_out, 8))
                for e in range(4):
                    r = nc.tensor.transpose(side[g][:, e * P:(e + 1) * P], XT[:, g, e, :], ident)
                r.then_inc(x1_mm, 1)

            def evens(ap, s):
                return ap.rearrange("p (b two s) -> p b two s", two=2, s=s)[:, :, 0, :]

            def lvP(l, i):
                lv, g = divmod(i, 4)
                s = SIZES[lv]
                if lv == 0:
                    pe.wait_ge(x1_out, due(l, x1_out, g + 1))
                else:
                    pe.wait_ge(lv_t_out, due(l, lv_t_out, i - 3))
                for e in range(4):
                    r = mm(side[g][:, e * 64:(e + 1) * 64], LT[:, g, e, :], evens(X[:, g, e, :], s), start=True, stop=True)
                r.then_inc(lv_p, 1)

            def lvV(l, i):
                g = i % 4
                pe.wait_ge(lv_p_out, due(l, lv_p_out, i + 1))
                for e in range(4):
                    r = mm(side[g][:, e * 64:(e + 1) * 64], XT[:, g, e, :], PB[:, g, e, :], start=True, stop=True)
                r.then_inc(lv_v, 1)

            def lvT(l, i):
                g = i % 4
                pe.wait_ge(lv_x, due(l, lv_x, i + 1))
                for e in range(4):
                    r = nc.tensor.transpose(side[g][:, e * P:(e + 1) * P], X[:, g, e, :], ident)
                r.then_inc(lv_t, 1)

            def t_v0(l, half):
                pe.wait_ge(lv_t_out, due(l, lv_t_out, 20 + half + 1))
                for e in range(4):
                    r = mm(side[half][:, e * P:(e + 1) * P], XT[:, half, e, :], vtok[:, 0, 4 * half + e, :],
                           start=True, stop=True)
                r.then_inc(t_v0m, 1)

            def t_st(l, half):
                pe.wait_ge(t_v0o, due(l, t_v0o, half + 1))
                pe.wait_ge(lv_t_out, due(l, lv_t_out, 22 + half + 1))
                for e in range(4):
                    h = 4 * half + e
                    r = mm(side[2 + half][:, e * P:(e + 1) * P], ktok[:, h, :], vn0[:, h, :], start=True, stop=True)
                r.then_inc(t_stm, 1)

            def t_ks(l, half):
                pe.wait_ge(t_sto, due(l, t_sto, half + 1))
                for e in range(4):
                    h = 4 * half + e
                    r = mm(side[half][:, e * P:(e + 1) * P], kT[:, h, P:2 * P], st[:, h, :], start=True, stop=True)
                r.then_inc(t_ksm, 1)

            def t_v1(l, half):
                pe.wait_ge(t_kso, due(l, t_kso, half + 1))
                for e in range(4):
                    h = 4 * half + e
                    r = mm(side[2 + half][:, e * P:(e + 1) * P], XT[:, 2 + half, e, :], rr[:, h, :], start=True, stop=True)
                r.then_inc(t_v1m, 1)

            def t_o(l, half):
                pe.wait_ge(t_v1o, due(l, t_v1o, half + 1))
                pe.wait_ge(qd_out, due(l, qd_out, 2))
                for e in range(4):
                    h = 4 * half + e
                    cols = slice(e * P, (e + 1) * P)
                    mm(side[half][:, cols], vn0[:, h, :], AT[:, half, e, :], start=True, stop=True)
                    mm(side[2 + half][:, cols], st[:, h, :], qd[:, h, :], start=True, stop=False)
                    r = mm(side[2 + half][:, cols], vn1[:, h, :], AT[:, 2 + half, e, :], start=False, stop=True)
                r.then_inc(t_om, 1)

            def onrm(l, i):
                pe.wait_ge(on_sq, due(l, on_sq, i + 1))
                if i < 2:
                    pe.wait_ge(t_oo, due(l, t_oo, 2))
                else:
                    pe.wait_ge(on_r, due(l, on_r, 2 * (i - 2) + 1))
                mm(side[i % 2][:], ones, sq[i % 2][:], start=True, stop=True).then_inc(on_mm, 1)

            def qrope(l, i):
                if i == 0:
                    pe.wait_ge(kr_out, due(l, kr_out, 2))
                else:
                    pe.wait_ge(qr_b, due(l, qr_b, 2 * i - 1))
                pe.wait_ge(act_evac, l * NACT_EVAC + evacs_through(FIRST["uq"] + 4 + i)[1])
                mm(side[4][:], perm, qr[:, 2 * i:2 * i + 2, :], start=True, stop=True).then_inc(qr_mm, 1)

            def sc(l, n):
                qt, hs = unit(n)
                w = P * (qt + 1)
                if n == 0:
                    pe.wait_ge(on_r, due(l, on_r, 8))
                    pe.wait_ge(kr_out, due(l, kr_out, 2))
                    pe.wait_ge(qr_out, due(l, qr_out, 2))
                    pe.wait_ge(act_evac, l * NACT_EVAC + evacs_through(FIRST["vt"] + 3)[1])
                elif n >= 2:
                    pe.wait_ge(sm_mask, due(l, sm_mask, n - 1))
                for e, h in enumerate(hs):
                    o_ = side[n % 2][:, e * w:(e + 1) * w]
                    mm(o_, qn[:, h, qt * P:(qt + 1) * P], kn[:, h, 0:w], start=True, stop=False)
                    r = mm(o_, qr[:, h // 2, qt * P:(qt + 1) * P], krz[:, h % 2, 0:w],
                           start=False, stop=True)
                r.then_inc(sc_mm, 1)

            def tr(l, n):
                pe.wait_ge(sm_out, due(l, sm_out, n + 1))
                if n >= 1:
                    pe.wait_ge(tr_out, due(l, tr_out, n))
                for e in range(4):
                    r = nc.tensor.transpose(side[2][:, e * P:(e + 1) * P], E[n % 2][:, e * P:(e + 1) * P], ident)
                r.then_inc(tr_mm, 1)

            def pv(l, n):
                qt, hs = unit(n)
                pe.wait_ge(tr_out, due(l, tr_out, n + 1))
                if n >= 2:
                    pe.wait_ge(pv_lo, due(l, pv_lo, n - 1))
                for e, h in enumerate(hs):
                    o_ = side[3 + n % 2][:, e * P:(e + 1) * P]
                    for kt in range(qt + 1):
                        p_ = PT[n % 2][:, (e * (qt + 1) + kt) * P:(e * (qt + 1) + kt + 1) * P]
                        r = mm(o_, vt[:, kt, h, :], p_, start=(kt == 0), stop=(kt == qt))
                r.then_inc(pv_mm, 1)

            def ysum(l, i):
                w, c = divmod(i, 4)
                pe.wait_ge(y_sq, due(l, y_sq, i + 1))
                for e in range(2):
                    r = mm(side[1][:, 0:S], ones, sq[i % 2][:, e * S:(e + 1) * S], start=(c == 0 and e == 0),
                           stop=(c == 3 and e == 1))
                r.then_inc(y_mm, 1)

            do = dict(pre=pre, ab=ab, logits=logits, dt=dt, job=job, gc=gc, vtrans=vtrans, nrm=nrm, latn=latn, ktrans=ktrans, decay=decay, x1=x1,
                      lvP=lvP, lvV=lvV, lvT=lvT, t_v0=t_v0, t_st=t_st, t_ks=t_ks, t_v1=t_v1, t_o=t_o, onrm=onrm,
                      sc=sc, tr=tr, pv=pv, ysum=ysum, qrope=qrope)
            with pe.Fori(0, DEPTH) as l:
                for what, n in ORDER:
                    if what in do:
                        do[what](l, n)

        @block.scalar
        def _(act):
            A = nc.scalar.activation

            def copy(o_, i_):
                return A(o_, i_, ACT.Copy)

            def split_hi(l, n):
                s = n % RING
                w = piece_width(n)
                act.wait_ge(loaded[s], (l * (NPIECE // RING) + n // RING + 1) * 16)
                act.wait_ge(steps_done, l * NSTEP + steps_through(n - RING) + RING)
                copy(whi[s][:, 0:w], raw[s][:, 0:w]).then_inc(hi_ready, 1)

            def rsqrt(l, rises, n, out_, in_, scale, bias_exp):
                A(out_, in_, ACT.Ln, scale=scale, bias=eps_col).then_inc(rises, 1)
                act.wait_ge(rises, due(l, rises, 2 * n + 1))
                A(out_, out_, ACT.Exp, scale=-0.5, bias=bias_exp).then_inc(rises, 1)

            def start(l, _):
                act.wait_ge(prm_ready, due(l, prm_ready, 1))
                copy(ab_hi[:], ab_all[:, l, :]).then_inc(ab_split_hi, 1)
                A(sm[:, 12, 0:H], prm[:, ALOG:ALOG + H], ACT.Exp).then_inc(ab_a, 1)

            def pre(l, w):
                t_, u_, q_ = (futmp, fuh, fusq) if w else (utmp, uh, usq)
                for c in range(4):
                    pair = slice(2 * c, 2 * c + 2)
                    x_pair = x_by_dve if c % 2 else x_by_pool
                    act.wait_ge(x_pair, due(l, x_pair, 1 + 2 * w + c // 2))
                    A(q_[:, pair, :], xT[:, pair, :], ACT.Square).then_inc(squared, 1)
                act.wait_ge(sumsq, due(l, sumsq, w + 1))
                rsqrt(l, rnorm, w, rn[1][:, 0:S], side[0][:, 0:S], 1.0 / D, 0.0)
                for c in range(4):
                    pair = slice(2 * c, 2 * c + 2)
                    act.wait_ge(pre_scaled, due(l, pre_scaled, 4 * w + c + 1))
                    copy(u_[:, pair, :], t_[:, pair, :]).then_inc(u_hi, 1)

            def logits(l, _):
                act.wait_ge(ab_z, due(l, ab_z, 2))
                A(sm[:, 1, :], sm[:, 0, :], ACT.Abs).then_inc(ab_abs, 1)
                act.wait_ge(ab_abs, due(l, ab_abs, 1))
                A(sm[:, 2, :], sm[:, 1, :], ACT.Exp, scale=-1.0).then_inc(ab_ex, 1)
                act.wait_ge(ab_w, due(l, ab_w, 1))
                A(sm[:, 4, :], sm[:, 3, :], ACT.Ln).then_inc(ab_ln, 1)
                act.wait_ge(ab_sp, due(l, ab_sp, 3))
                A(sm[:, 8, :].rearrange("p (t n) -> p t n", t=NT)[:, :, 8:16],
                  sm[:, 7, :].rearrange("p (t n) -> p t n", t=NT)[:, :, 8:16], ACT.Exp, scale=-1.0).then_inc(ab_a, 1)

            def job(l, j):
                kind, i, _ = JOBS[j]
                bank = dense[j % 3]
                if kind not in EVAC_BY_ACT and kind not in ("out", "ff2"):
                    return
                act.wait_ge(steps_done, products_done(l, j))
                pair = slice(2 * i, 2 * i + 2)
                if kind in ("v", "q", "k"):
                    n = j
                    dst, chunk0 = conv_place(n)
                    for c in range(2):
                        x_ = A(dst[:, 2 * (n % 4) + c, :], bank[:, c * S:(c + 1) * S], ACT.Identity,
                               scale=prm[:, CONV + 3 * (QKV // P) + chunk0 + c:CONV + 3 * (QKV // P) + chunk0 + c + 1])
                    x_.then_inc(tap0, 1)
                    if n >= 2:
                        act.wait_ge(conv_mid, due(l, conv_mid, 6 * (n - 1)))
                    copy(cb[n % 2][:], bank[:]).then_inc(act_evac, 1)
                elif kind == "lat":
                    if i < 2:
                        A(sq_kv[:] if i == 0 else sq_q[:, 0:512], bank[:], ACT.Square).then_inc(lat_sq, 1)
                        copy(latT[:, pair, :], bank[:]).then_inc(act_evac, 1)
                    else:
                        A(sq_q[:, 512:768], bank[:, 0:S], ACT.Square).then_inc(lat_sq, 1)
                        copy(latT[:, 4, :], bank[:, 0:S])
                        copy(krx[:], bank[:, S:2 * S]).then_inc(act_evac, 1)
                elif kind == "uq":
                    dst = qn[:, pair, :] if i < 4 else qr[:, 2 * (i - 4):2 * (i - 4) + 2, :]
                    copy(dst, bank[:]).then_inc(act_evac, 1)
                elif kind == "kn":
                    copy(kn[:, pair, :], bank[:]).then_inc(act_evac, 1)
                elif kind == "vt":
                    h0 = 4 * (i // 2)
                    copy(vt[:, i % 2, h0:h0 + 4, :], bank[:]).then_inc(act_evac, 1)
                elif kind == "z":
                    if i == 0:
                        act.wait_ge(qd_out, due(l, qd_out, 2))
                    A(zs[:, pair, :], bank[:], ACT.Silu).then_inc(act_evac, 1)
                elif kind in ("out", "ff2"):
                    n = i + (4 if kind == "ff2" else 0)
                    if i >= 2:
                        act.wait_ge(y_mm, due(l, y_mm, n - 1))
                    A(sq[i % 2][:], bank[:], ACT.Square).then_inc(y_sq, 1)

            def silu(l, n):
                dst = conv_place(n)[0][:, 2 * (n % 4):2 * (n % 4) + 2, :]
                act.wait_ge(conv_mid, due(l, conv_mid, 6 * (n + 1)))
                A(dst, dst, ACT.Silu).then_inc(silu_done, 1)

            def vtrans(l, i):
                t, half = i // 2, i % 2
                act.wait_ge(vtrans_mm, due(l, vtrans_mm, i + 1))
                copy(vtok[:, t, 4 * half:4 * half + 4, :], side[3 + i % 2][:]).then_inc(vtrans_out, 1)

            def lnexp(l, i):
                nc.scalar.preload_act_table_set("natural_log_exp_and_others")
                if i == 0:
                    act.wait_ge(gc_copied, due(l, gc_copied, 3))
                    A(sm[:, 11, :], sm[:, 9, :], ACT.Exp).then_inc(gc_exp, 1)
                    A(sm[:, 13, :], sm[:, 10, :], ACT.Exp).then_inc(gc_exp, 1)
                    act.wait_ge(vtrans_mm, due(l, vtrans_mm, 4))
                    for g, bank in ((2, side[2]), (3, side[0])):
                        act.wait_ge(dt_arg, due(l, dt_arg, g + 1))
                        A(qd[:, 4 * (g - 2):4 * (g - 1), :], bank[:], ACT.Exp).then_inc(dec_eg, 1)
                    for g in range(4):
                        A(DT[:, g], DT[:, g], ACT.Exp).then_inc(dec_exp, 1)

            def nrm(l, i):
                act.wait_ge(nrm_mm, due(l, nrm_mm, i + 1))
                if i >= 2:
                    act.wait_ge(nrm_out, due(l, nrm_out, i - 1))
                rsqrt(l, nrm_r, i, rn[i % 2][:], side[1 + 2 * (i % 2)][:], 1.0, lnscale_col if i < 4 else 0.0)

            def latn(l, i):
                if i == 1:
                    return
                n = 0 if i == 0 else 1
                act.wait_ge(lat_mm, due(l, lat_mm, n + 1))
                if n:
                    act.wait_ge(lat_norm, due(l, lat_norm, 2))
                rsqrt(l, lat_r, n, rl[:], side[4][:, 0:S], 1.0 / (QL if n else KVL), 0.0)
                a_, b_ = (2, 5) if n else (0, 2)
                act.wait_ge(lat_norm, due(l, lat_norm, 5 if n else 2))
                copy(lath[:, a_:b_, :], latT[:, a_:b_, :]).then_inc(lat_hi, 1)

            def x1(l, g):
                act.wait_ge(x1_mm, due(l, x1_mm, g + 1))
                copy(X[:, g], side[g][:]).then_inc(x1_out, 1)

            def lvT(l, i):
                act.wait_ge(lv_t, due(l, lv_t, i + 1))
                copy(XT[:, i % 4], side[i % 4][:]).then_inc(lv_t_out, 1)

            def t_st(l, half):
                act.wait_ge(t_stm, due(l, t_stm, half + 1))
                copy(st[:, 4 * half:4 * half + 4, :], side[2 + half][:]).then_inc(t_sto, 1)

            def t_o(l, half):
                hs = slice(4 * half, 4 * half + 4)
                act.wait_ge(t_om, due(l, t_om, half + 1))
                copy(oT[:, hs, 0:P], side[half][:])
                copy(oT[:, hs, P:2 * P], side[2 + half][:]).then_inc(t_oo, 1)

            def onrm(l, i):
                act.wait_ge(on_mm, due(l, on_mm, i + 1))
                if i >= 2:
                    act.wait_ge(on_o, due(l, on_o, i - 1))
                rsqrt(l, on_r, i, rn[i % 2][:], side[i % 2][:], 1.0 / DK, 0.0)

            def osplit(l, i):
                act.wait_ge(on_z, due(l, on_z, i + 1))
                copy(oh[:, 2 * i:2 * i + 2, :], oT[:, 2 * i:2 * i + 2, :]).then_inc(on_hi, 1)

            def sc(l, n):
                act.wait_ge(sm_sub, due(l, sm_sub, n + 1))
                A(E[n % 2][:], E[n % 2][:], ACT.Exp, scale=float((DK + ROPE) ** -0.5)).then_inc(sm_exp, 1)

            def tr(l, n):
                act.wait_ge(tr_mm, due(l, tr_mm, n + 1))
                if n >= 2:
                    act.wait_ge(pv_mm, due(l, pv_mm, n - 1))
                copy(PT[n % 2][:], side[2][:]).then_inc(tr_out, 1)

            def pv(l, n):
                qt, hs = unit(n)
                nh = len(hs)
                act.wait_ge(pv_mm, due(l, pv_mm, n + 1))
                copy(ah[:, hs[0]:hs[0] + nh, qt * P:(qt + 1) * P], side[3 + n % 2][:, 0:nh * P]).then_inc(pv_hi, 1)

            def sig(l, _):
                nc.scalar.preload_act_table(ACT.Sigmoid)
                act.wait_ge(dve_evac, l * NDVE_EVAC + evacs_through(FIRST["gate"] + 7)[1])
                flat = gates[:].rearrange("p b c s -> p (b c s)")
                for i in range(4):
                    part = flat[:, i * 1024:(i + 1) * 1024]
                    A(part, part, ACT.Sigmoid).then_inc(sig_done, 1)
                nc.scalar.preload_act_table_set("natural_log_exp_and_others")

            def hsplit(l, i):
                act.wait_ge(h_sum, due(l, h_sum, i + 1))
                copy(hh[:, 2 * i:2 * i + 2, :], hA[:, 2 * i:2 * i + 2, :]).then_inc(h_hi, 1)

            def post(l, w):
                act.wait_ge(y_mm, due(l, y_mm, 4 * w + 4))
                rsqrt(l, y_r, w, rn[0][:, 0:S], side[1][:, 0:S], 1.0 / D, 0.0)

            def fsplit(l, i):
                act.wait_ge(f_sq, due(l, f_sq, i + 1))
                copy(fh[:, 2 * i:2 * i + 2, :], fr[i % 4][:]).then_inc(f_hi, 1)

            do = dict(start=start, pre=pre, logits=logits, job=job, silu=silu, vtrans=vtrans, lnexp=lnexp, nrm=nrm, latn=latn,
                      x1=x1, lvT=lvT, t_st=t_st, t_o=t_o, onrm=onrm, osplit=osplit, sc=sc, tr=tr, pv=pv, sig=sig,
                      hsplit=hsplit, post=post, fsplit=fsplit)
            act.wait_ge(s_in, 5 * 16)
            act.wait_ge(s_trig, 12)
            A(cosT[:], ang[:, 0, :], ACT.Sin).then_inc(s_trig_a, 1)
            act.wait_ge(s_trig, 20)
            A(sinT[:], ang[:, 1, :], ACT.Sin).then_inc(s_trig_a, 1)
            with act.Fori(0, DEPTH) as l:
                nc.scalar.preload_act_table_set("natural_log_exp_and_others")
                for (what, n), pieces in zip(ORDER, splits_at):
                    for p_ in pieces:
                        split_hi(l, p_)
                    if what in do:
                        do[what](l, n)

        @block.vector
        def _(dve):
            V = nc.vector
            TT, TS, STT = V.tensor_tensor, V.tensor_scalar, V.scalar_tensor_tensor
            dve.sem_inc(lo_ready, RING)
            dve.sem_inc(x_by_dve, 2)

            def f32(ap):
                return ap.bitcast(F32)

            def split_lo(l, n):
                s = n % RING
                w = piece_width(n)
                dve.wait_ge(hi_ready, l * NPIECE + n + 1)
                TT(wlo[s][:, 0:w], raw[s][:, 0:w], f32(whi[s][:, 0:w]), ALU.subtract).then_inc(lo_ready, 1)

            def col(n):
                return prm[:, n:n + 1]

            def start(l, _):
                dve.wait_ge(x_by_pool, due(l, x_by_pool, 2))
                V.tensor_copy(prm[:], prm_all[:, l, :]).then_inc(prm_ready, 1)
                dve.wait_ge(ab_split_hi, due(l, ab_split_hi, 1))
                TT(ab_lo[:], ab_all[:, l, :], f32(ab_hi[:]), ALU.subtract).then_inc(ab_split_lo, 1)

            def pre(l, w):
                t_, uh_, ul_ = (futmp, fuh, ful) if w else (utmp, uh, ul)
                dve.wait_ge(prm_ready, due(l, prm_ready, 1))
                dve.wait_ge(x_by_pool, due(l, x_by_pool, 2 + 2 * w))
                dve.wait_ge(x_by_dve, due(l, x_by_dve, 2 + 2 * w))
                for c in range(KD):
                    x_ = TS(t_[:, c, :], xT[:, c, :], col((PRE_FFN if w else PRE_MIX) + c), None, ALU.mult)
                x_.then_inc(weighted, 1)
                dve.wait_ge(weighted, due(l, weighted, w + 1))
                dve.wait_ge(rnorm, due(l, rnorm, 2 * w + 2))

                def low(c):
                    pair = slice(2 * c, 2 * c + 2)
                    dve.wait_ge(u_hi, due(l, u_hi, 4 * w + c + 1))
                    TT(ul_[:, pair, :], t_[:, pair, :], f32(uh_[:, pair, :]), ALU.subtract).then_inc(u_lo, 1)

                for c in range(4):
                    pair = slice(2 * c, 2 * c + 2)
                    TT(t_[:, pair, :], t_[:, pair, :], over_heads(rn[1][:, 0:S], 2), ALU.mult).then_inc(pre_scaled, 1)
                    if c >= 1:
                        low(c - 1)
                low(3)

            def ab(l, _):
                dve.wait_ge(ab_t, due(l, ab_t, 1))
                V.tensor_copy(abT[:], side[1][0:16, 0:S]).then_inc(ab_t_copied, 1)

            def logits(l, _):
                by_t = lambda n: sm[:, n, :].rearrange("p (t n) -> p t n", t=NT)
                over_t = lambda ap: ap.rearrange("p (a n) -> p a n", a=1).broadcast_to([P, NT, H])
                dve.wait_ge(ab_mm, due(l, ab_mm, 1))
                raw_ = side[2][:, 0:32].rearrange("p (t n) -> p t n", t=NT)
                TT(by_t(0)[:, :, 0:8], raw_[:, :, 0:8], over_t(prm[:, DTB:DTB + H]), ALU.add).then_inc(ab_z, 1)
                TS(by_t(0)[:, :, 8:16], raw_[:, :, 8:16], -1.0, None, ALU.mult).then_inc(ab_z, 1)
                dve.wait_ge(ab_ex, due(l, ab_ex, 1))
                TS(sm[:, 3, :], sm[:, 2, :], 1.0, None, ALU.add).then_inc(ab_w, 1)
                dve.wait_ge(ab_w, due(l, ab_w, 1))
                STT(sm[:, 5, :], sm[:, 3, :], -1.0, sm[:, 2, :], ALU.add, ALU.subtract).then_inc(ab_w, 1)
                V.reciprocal(sm[:, 6, :], sm[:, 3, :]).then_inc(ab_rc, 1)
                dve.wait_ge(ab_w, due(l, ab_w, 2))
                dve.wait_ge(ab_rc, due(l, ab_rc, 1))
                TT(sm[:, 5, :], sm[:, 5, :], sm[:, 6, :], ALU.mult).then_inc(ab_sp, 1)
                dve.wait_ge(ab_sp, due(l, ab_sp, 1))
                dve.wait_ge(ab_ln, due(l, ab_ln, 1))
                TT(sm[:, 7, :], sm[:, 4, :], sm[:, 5, :], ALU.subtract).then_inc(ab_sp, 1)
                dve.wait_ge(ab_sp, due(l, ab_sp, 2))
                STT(sm[:, 7, :], sm[:, 0, :], 0.0, sm[:, 7, :], ALU.max, ALU.add).then_inc(ab_sp, 1)
                dve.wait_ge(ab_sp, due(l, ab_sp, 3))
                dve.wait_ge(ab_a, due(l, ab_a, 1))
                STT(by_t(8)[:, :, 0:8], by_t(7)[:, :, 0:8], -1.0, over_t(sm[:, 12, 0:H]), ALU.mult,
                    ALU.mult).then_inc(ab_g, 1)

            def gc(l, _):
                dve.wait_ge(gc_mm, due(l, gc_mm, 1))
                V.tensor_copy(sm[:, 9, :], side[2][:, 0:32]).then_inc(gc_copied, 1)
                V.tensor_copy(gcT[:], side[2][0:8, 128:384]).then_inc(gc_copied, 1)
                dve.wait_ge(gc_copied, due(l, gc_copied, 1))
                TT(sm[:, 10, :], side[2][:, 32:64], sm[:, 9, :], ALU.subtract).then_inc(gc_copied, 1)

            def conv(l, n):
                dst, chunk0 = conv_place(n)
                dve.wait_ge(tap0, due(l, tap0, n + 1))
                dve.wait_ge(act_evac, l * NACT_EVAC + n + 1)
                for back in range(1, 4):
                    for c in range(2):
                        m = 2 * (back - 1) + c
                        y_, x_ = dst[:, 2 * (n % 4) + c, back:], cb[n % 2][:, c, 0:S - back]
                        if back > 1:
                            dve.wait_ge(conv_mid, due(l, conv_mid, 6 * n + m - 1))
                        STT(y_, x_, col(CONV + (3 - back) * (QKV // P) + chunk0 + c), y_, ALU.mult,
                            ALU.add).then_inc(conv_mid, 1)

            def dt(l, g):
                dve.wait_ge(dt_mm, due(l, dt_mm, g + 1))
                dve.wait_ge(dt_fut, due(l, dt_fut, g + 1))
                TT(DT[:, g], heads4(side[g % 3][:]), DT[:, g], ALU.add).then_inc(dt_arg, 1)

            def nrm(l, i):
                dst = [qT, kT][i // 4][:, 2 * (i % 4):2 * (i % 4) + 2, :]
                dve.wait_ge(nrm_r, due(l, nrm_r, 2 * i + 2))
                TT(dst, dst, rn[i % 2][:].rearrange("p (c s) -> p c s", c=2), ALU.mult).then_inc(nrm_out, 1)

            def latn(l, i):
                if i == 1:
                    return
                n = 0 if i == 0 else 1
                a_, b_ = (2, 5) if n else (0, 2)
                dve.wait_ge(lat_r, due(l, lat_r, 2 * n + 2))
                for c in range(a_, b_):
                    STT(latT[:, c, :], latT[:, c, :], col(QA + c - 2 if n else KVA + c), rl[:], ALU.mult,
                        ALU.mult).then_inc(lat_norm, 1)
                dve.wait_ge(lat_hi, due(l, lat_hi, n + 1))
                TT(latl[:, a_:b_, :], latT[:, a_:b_, :], f32(lath[:, a_:b_, :]), ALU.subtract).then_inc(lat_lo, 1)
                if n:
                    dve.wait_ge(kr_mm, due(l, kr_mm, 1))
                    TT(kr[:], side[4][:, S:2 * S], sinT[:], ALU.mult).then_inc(kr_b, 1)
                    TT(kra[:], krx[:], cosT[:], ALU.mult).then_inc(kr_b, 1)
                    dve.wait_ge(kr_b, due(l, kr_b, 2))
                    TT(kr[:], kr[:], kra[:], ALU.add).then_inc(kr_b, 1)
                    dve.wait_ge(kr_b, due(l, kr_b, 3))
                    for e in range(2):
                        TS(krz[:, e, :], kr[:], cst[:, C_FREQ + 2 + e:C_FREQ + 3 + e], None, ALU.mult).then_inc(kr_out, 1)

            def qrope(l, i):
                q_ = qr[:, 2 * i:2 * i + 2, :]
                tmp = sq[i][:].rearrange("p (c s) -> p c s", c=2)
                dve.wait_ge(qr_mm, due(l, qr_mm, i + 1))
                TT(tmp, side[4][:].rearrange("p (c s) -> p c s", c=2), over_heads(sinT[:], 2), ALU.mult).then_inc(qr_b, 1)
                TT(q_, q_, over_heads(cosT[:], 2), ALU.mult).then_inc(qr_b, 1)
                dve.wait_ge(qr_b, due(l, qr_b, 2 * i + 2))
                TT(q_, q_, tmp, ALU.add).then_inc(qr_out, 1)

            def heads4(ap):
                return ap.rearrange("p (e c) -> p e c", e=4)

            def small(slot, t, h0, first=0):
                a_ = 16 * t + first + h0
                return sm[:, slot, a_:a_ + 4]

            def ktrans(l, half):
                dve.wait_ge(ktrans_mm, due(l, ktrans_mm, half + 1))
                dve.wait_ge(gc_exp, due(l, gc_exp, 2))
                TT(ktok[:, 4 * half:4 * half + 4, :], heads4(side[2 + half][:]), along(small(13, 0, 4 * half), P),
                   ALU.mult).then_inc(ktrans_out, 1)

            def decay(l, g):
                b_ = 2 * (g % 2)
                dve.wait_ge(dec_mm, due(l, dec_mm, g + 1))
                dve.wait_ge(dec_exp, due(l, dec_exp, g + 1))
                for e, h in enumerate(heads_of(g)):
                    beta = sm[:, 8, 16 * (g // 2) + 8 + h:16 * (g // 2) + 9 + h]
                    x_ = STT(LT[:, g, e, :], side[b_][:, e * P:(e + 1) * P], beta, DT[:, g, e, :], ALU.mult, ALU.mult)
                x_.then_inc(dec_out, 1)
                TT(AT[:, g], heads4(side[b_ + 1][:]), DT[:, g], ALU.mult).then_inc(dec_out, 1)

            def lvP(l, i):
                lv, g = divmod(i, 4)
                mask = cst[:, C_LV + 64 * lv:C_LV + 64 * (lv + 1)]
                dve.wait_ge(lv_p, due(l, lv_p, i + 1))
                TT(PB[:, g], side[g][:, 0:256].rearrange("p (e c) -> p e c", e=4), over_heads(mask, 4),
                   ALU.mult).then_inc(lv_p_out, 1)

            def lvV(l, i):
                lv, g = divmod(i, 4)
                s = SIZES[lv]
                dve.wait_ge(lv_v, due(l, lv_v, i + 1))
                x_ = X[:, g].rearrange("p e (b two s) -> p (e b) two s", two=2, s=s)[:, :, 0, :]
                TT(x_, x_, side[g][:, 0:256].rearrange("p (b s) -> p b s", s=s), ALU.subtract).then_inc(lv_x, 1)

            def t_v0(l, half):
                dve.wait_ge(t_v0m, due(l, t_v0m, half + 1))
                TT(vn0[:, 4 * half:4 * half + 4, :], heads4(side[half][:]), along(small(8, 0, 4 * half, 8), P),
                   ALU.mult).then_inc(t_v0o, 1)

            def t_v1(l, half):
                dve.wait_ge(t_v1m, due(l, t_v1m, half + 1))
                TT(vn1[:, 4 * half:4 * half + 4, :], heads4(side[2 + half][:]), along(small(8, 1, 4 * half, 8), P),
                   ALU.mult).then_inc(t_v1o, 1)

            def t_ks(l, half):
                hs = slice(4 * half, 4 * half + 4)
                dve.wait_ge(t_ksm, due(l, t_ksm, half + 1))
                TT(rr[:, hs, :], heads4(side[half][:]), along(small(11, 1, 4 * half), P), ALU.mult).then_inc(t_kst, 1)
                dve.wait_ge(t_kst, due(l, t_kst, half + 1))
                TT(rr[:, hs, :], vtok[:, 1, hs, :], rr[:, hs, :], ALU.subtract).then_inc(t_kso, 1)

            def onrm(l, i):
                o_ = oT[:, 2 * i:2 * i + 2, :].rearrange("p c s -> p (c s)")
                dve.wait_ge(on_r, due(l, on_r, 2 * i + 2))
                STT(o_, o_, col(GDN), rn[i % 2][:], ALU.mult, ALU.mult).then_inc(on_o, 1)

            def osplit(l, i):
                p_ = slice(2 * i, 2 * i + 2)
                dve.wait_ge(on_hi, due(l, on_hi, i + 1))
                TT(ol[:, p_, :], oT[:, p_, :], f32(oh[:, p_, :]), ALU.subtract).then_inc(on_lo, 1)

            def sc(l, n):
                qt, hs = unit(n)
                nh, w = len(hs), P * (qt + 1)
                e_ = E[n % 2][:].rearrange("p (e c) -> p e c", e=nh)
                mask = amask[:, P * (1 - qt):2 * P]
                dve.wait_ge(sc_mm, due(l, sc_mm, n + 1))
                if n >= 2:
                    dve.wait_ge(tr_mm, due(l, tr_mm, n - 1))
                TT(e_, side[n % 2][:].rearrange("p (e c) -> p e c", e=nh), over_heads(mask, nh), ALU.add).then_inc(sm_mask, 1)
                dve.wait_ge(sm_mask, due(l, sm_mask, n + 1))
                V.tensor_reduce(mx[:, 0:nh], e_, AX, ALU.max).then_inc(sm_max, 1)
                dve.wait_ge(sm_max, due(l, sm_max, n + 1))
                TT(e_, e_, along(mx[:, 0:nh], w), ALU.subtract).then_inc(sm_sub, 1)
                dve.wait_ge(sm_exp, due(l, sm_exp, n + 1))
                V.tensor_reduce(mx[:, 0:nh], e_, AX, ALU.add).then_inc(sm_sum, 1)
                dve.wait_ge(sm_sum, due(l, sm_sum, n + 1))
                V.reciprocal(rs[:, 0:nh], mx[:, 0:nh]).then_inc(sm_rec, 1)
                dve.wait_ge(sm_rec, due(l, sm_rec, n + 1))
                TT(e_, e_, along(rs[:, 0:nh], w), ALU.mult).then_inc(sm_out, 1)

            def pv(l, n):
                qt, hs = unit(n)
                nh = len(hs)
                dve.wait_ge(pv_hi, due(l, pv_hi, n + 1))
                where = (slice(None), slice(hs[0], hs[0] + nh), slice(qt * P, (qt + 1) * P))
                TT(al[where], side[3 + n % 2][:, 0:nh * P].rearrange("p (e c) -> p e c", e=nh), f32(ah[where]),
                   ALU.subtract).then_inc(pv_lo, 1)

            def job(l, j):
                kind, i, _ = JOBS[j]
                bank = dense[j % 3]
                if kind in EVAC_BY_ACT:
                    return
                dve.wait_ge(steps_done, products_done(l, j))
                pair = slice(2 * (i % 4), 2 * (i % 4) + 2)
                b2 = bank[:].rearrange("p (c s) -> p c s", c=2)
                if kind == "gate":
                    V.tensor_copy(gates[:, i // 4, pair, :], b2).then_inc(dve_evac, 1)
                elif kind == "ya":
                    dve.wait_ge(sig_done, due(l, sig_done, 4))
                    TT(hA[:, pair, :], b2, gates[:, 0, pair, :], ALU.mult).then_inc(dve_evac, 1)
                elif kind in ("out", "ff2"):
                    w = kind == "ff2"
                    dve.wait_ge(y_sq, due(l, y_sq, 4 * w + i + 1))
                    for c in range(2):
                        x_ = TS(yT[:, 2 * i + c, :], bank[:, c * S:(c + 1) * S], col((POST_FFN if w else POST_MIX) + 2 * i + c),
                                None, ALU.mult)
                    x_.then_inc(dve_evac, 1)
                elif kind == "yb":
                    TT(hB[i % 2][:].rearrange("p (c s) -> p c s", c=2), b2, gates[:, 1, pair, :],
                       ALU.mult).then_inc(dve_evac, 1)
                    dve.wait_ge(dve_evac, l * NDVE_EVAC + evacs_through(j)[1])
                    TT(hA[:, pair, :], hA[:, pair, :], hB[i % 2][:].rearrange("p (c s) -> p c s", c=2),
                       ALU.add).then_inc(h_sum, 1)
                elif kind == "ff1":
                    TS(fr[i % 4][:], bank[:], 0.0, None, ALU.max).then_inc(dve_evac, 1)

            def hsplit(l, i):
                p_ = slice(2 * i, 2 * i + 2)
                dve.wait_ge(h_hi, due(l, h_hi, i + 1))
                TT(hl[:, p_, :], hA[:, p_, :], f32(hh[:, p_, :]), ALU.subtract).then_inc(h_lo, 1)

            def post(l, w):
                dve.wait_ge(y_r, due(l, y_r, 2 * w + 2))
                dve.wait_ge(dve_evac, l * NDVE_EVAC + evacs_through(FIRST["ff2" if w else "out"] + 3)[1])

                def times_norm(c):
                    pair = slice(2 * c, 2 * c + 2)
                    TT(yT[:, pair, :], yT[:, pair, :], over_heads(rn[0][:, 0:S], 2), ALU.mult).then_inc(y_scaled, 1)

                for c in (0, 2):
                    times_norm(c)
                    times_norm(c + 1)
                    dve.wait_ge(y_scaled, due(l, y_scaled, 4 * w + c + 2))
                    pair = slice(2 * c + 2, 2 * c + 4)
                    TT(xT[:, pair, :], xT[:, pair, :], yT[:, pair, :], ALU.add).then_inc(x_by_dve, 1)

            def fsplit(l, i):
                dve.wait_ge(f_hi, due(l, f_hi, i + 1))
                TT(fl[:, 2 * i:2 * i + 2, :], fr[i % 4][:].rearrange("p (c s) -> p c s", c=2),
                   f32(fh[:, 2 * i:2 * i + 2, :]), ALU.subtract).then_inc(f_lo, 1)

            do = dict(start=start, pre=pre, ab=ab, logits=logits, gc=gc, dt=dt, conv=conv, nrm=nrm, latn=latn, qrope=qrope, ktrans=ktrans,
                      decay=decay, lvP=lvP, lvV=lvV, t_v0=t_v0, t_v1=t_v1, t_ks=t_ks, onrm=onrm, osplit=osplit, sc=sc, pv=pv, job=job,
                      hsplit=hsplit, post=post, fsplit=fsplit)

            V.memset(eps_col, EPS).then_inc(s_trig, 1)
            V.memset(lnscale_col, math.log(DK ** -0.5)).then_inc(s_trig, 1)
            dve.wait_ge(s_in, 5 * 16)
            n_ = [2]

            def step(ins):
                n_[0] += 1
                ins.then_inc(s_trig, 1)
                dve.wait_ge(s_trig, n_[0])

            turn = 2.0 * math.pi
            t1 = 6.28125
            t2 = round((turn - t1) * 2 ** 22) / 2 ** 22
            t3 = turn - t1 - t2
            magic = 1.5 * 2 ** 23
            A_ = lambda i: ang[:, i, :]
            step(V.tensor_copy(A_(2), pos_i[:]))
            step(TS(A_(2), A_(2), cst[:, C_FREQ:C_FREQ + 1], None, ALU.mult))
            for dst, shift, add in ((0, 0.25, 0.5 * math.pi), (1, 0.0, 0.0)):
                step(TS(A_(3), A_(2), 1.0 / turn, shift, ALU.mult, ALU.add))
                step(TS(A_(3), A_(3), magic, None, ALU.add))
                step(TS(A_(3), A_(3), magic, None, ALU.subtract))
                step(STT(A_(dst), A_(3), -t1, A_(2), ALU.mult, ALU.add))
                step(STT(A_(dst), A_(3), -t2, A_(dst), ALU.mult, ALU.add))
                step(STT(A_(dst), A_(3), -t3, A_(dst), ALU.mult, ALU.add))
                step(TS(A_(dst), A_(dst), add, None, ALU.add))
                step(TS(A_(dst), A_(dst), PI_BELOW, -PI_BELOW, ALU.min, ALU.max))
            dve.wait_ge(s_trig_a, 2)
            step(TS(sinT[:], sinT[:], cst[:, C_FREQ + 1:C_FREQ + 2], None, ALU.mult))

            with dve.Fori(0, DEPTH) as l:
                for (what, n), pieces in zip(ORDER, splits_at):
                    for p_ in pieces:
                        split_lo(l, p_)
                    if what in do:
                        do[what](l, n)

        @block.gpsimd
        def _(pool):
            G = nc.gpsimd.tensor_tensor

            def nrm(l, i):
                src = [qT, kT][i // 4][:, 2 * (i % 4):2 * (i % 4) + 2, :].rearrange("p c s -> p (c s)")
                pool.wait_ge(silu_done, due(l, silu_done, 5 + i))
                if i >= 2:
                    pool.wait_ge(nrm_mm, due(l, nrm_mm, i - 1))
                G(sq[i % 2][:], src, src, ALU.mult).then_inc(nrm_sq, 1)

            def dt(l, g):
                pool.wait_ge(gc_copied, due(l, gc_copied, 1))
                gc_m = sm[:, 9, 16 * (g // 2) + 4 * (g % 2):16 * (g // 2) + 4 * (g % 2) + 4]
                G(DT[:, g], over_heads(future, 4), along(gc_m, P), ALU.subtract).then_inc(dt_fut, 1)

            def latn(l, i):
                if i == 2:
                    for half in range(2):
                        hs = slice(4 * half, 4 * half + 4)
                        pool.wait_ge(dec_eg, due(l, dec_eg, half + 1))
                        pool.wait_ge(nrm_out, due(l, nrm_out, 4))
                        G(qd[:, hs, :], qT[:, hs, P:2 * P], qd[:, hs, :], ALU.mult).then_inc(qd_out, 1)

            def x1(l, g):
                pool.wait_ge(dec_out, due(l, dec_out, 2 * g + 2))
                G(XT[:, g], LT[:, g], over_heads(below1, 4), ALU.mult).then_inc(x1_mask, 1)
                pool.wait_ge(x1_mask, due(l, x1_mask, g + 1))
                G(XT[:, g], over_heads(ident, 4), XT[:, g], ALU.subtract).then_inc(x1_xt, 1)

            def onrm(l, i):
                src = oT[:, 2 * i:2 * i + 2, :].rearrange("p c s -> p (c s)")
                pool.wait_ge(t_oo, due(l, t_oo, 2))
                if i >= 2:
                    pool.wait_ge(on_mm, due(l, on_mm, i - 1))
                G(sq[i % 2][:], src, src, ALU.mult).then_inc(on_sq, 1)

            def osplit(l, i):
                o_ = oT[:, 2 * i:2 * i + 2, :].rearrange("p c s -> p (c s)")
                pool.wait_ge(on_o, due(l, on_o, i + 1))
                pool.wait_ge(act_evac, l * NACT_EVAC + evacs_through(FIRST["z"] + 3)[1])
                G(o_, o_, zs[:, 2 * i:2 * i + 2, :].rearrange("p c s -> p (c s)"), ALU.mult).then_inc(on_z, 1)

            def fsplit(l, i):
                pool.wait_ge(dve_evac, l * NDVE_EVAC + evacs_through(FIRST["ff1"] + i)[1])
                G(fr[i % 4][:], fr[i % 4][:], fr[i % 4][:], ALU.mult).then_inc(f_sq, 1)

            def post(l, w):
                for c in (0, 2):
                    pair = slice(2 * c, 2 * c + 2)
                    pool.wait_ge(y_scaled, due(l, y_scaled, 4 * w + c + 1))
                    G(xT[:, pair, :], xT[:, pair, :], yT[:, pair, :], ALU.add).then_inc(x_by_pool, 1)

            do = dict(nrm=nrm, dt=dt, latn=latn, x1=x1, onrm=onrm, osplit=osplit, fsplit=fsplit, post=post)
            pool.wait_ge(s_in, 5 * 16)
            pool.sem_inc(x_by_pool, 2)
            with pool.Fori(0, DEPTH) as l:
                for what, n in ORDER:
                    if what in do:
                        do[what](l, n)


def constants():
    c = np.zeros((P, NCST), np.float32)
    i = np.arange(P)
    c[:, C_ID:C_ID + P] = np.eye(P)
    c[:, C_UT:C_UT + P] = i[:, None] <= i[None, :]
    c[:, C_NEG:C_NEG + P] = np.where(i[:, None] > i[None, :], -1e30, 0.0)
    c[:, C_M1:C_M1 + P] = (i[None, :] % 2 == 1) & (i[:, None] == i[None, :] - 1)
    for lv, s in enumerate(SIZES):
        pair_of_column = np.arange(64) // s
        c[:, C_LV + 64 * lv:C_LV + 64 * (lv + 1)] = i[:, None] // s == 2 * pair_of_column[None, :] + 1
    c[:, C_ONE:C_ONE + P] = 1.0
    c[:, C_PERM:C_PERM + P] = i[:, None] == (i[None, :] ^ (ROPE // 2))
    c[:, C_AM + P:C_AM + 2 * P] = np.where(i[None, :] // CHUNK > i[:, None] // CHUNK, -1e30, 0.0)
    freq = np.float32(10000.0) ** (-np.arange(0, ROPE, 2, dtype=np.float32) / np.float32(ROPE))
    c[:, C_FREQ] = freq[i % (ROPE // 2)]
    c[:, C_FREQ + 2] = i < ROPE
    c[:, C_FREQ + 3] = i >= ROPE
    c[:, C_FREQ + 1] = np.where(i % ROPE < ROPE // 2, -1.0, 1.0)
    return c


def blocks(w, k0, kn_, cols):
    a = w[k0 * P:(k0 + kn_) * P][:, cols]
    return a.reshape(kn_, P, -1).transpose(1, 0, 2).reshape(P, -1)


def lay_out_weights(w_in, w_uq, w_ukv, w_a, w_b, w_out, w_ff1, w_ff2):
    q0, k0, v0 = 0, H * DK, 2 * H * DK
    z0 = QKV
    cq0 = z0 + H * DK + 2 * H
    ckv0, kr0 = cq0 + QL, cq0 + QL + KVL
    g0 = kr0 + ROPE
    r = np.arange
    pieces = []
    for lyr in range(DEPTH):
        def wide(w, cols, kd=KD):
            for h_ in range(kd // 4):
                pieces.append(blocks(w, 4 * h_, 4, cols))
        for start in (v0, q0, k0):
            for i in range(4):
                wide(w_in[lyr], start + 256 * i + r(256))
        krope = kr0 + r(ROPE)
        wide(w_in[lyr], ckv0 + r(256))
        wide(w_in[lyr], cq0 + r(256))
        wide(w_in[lyr], np.concatenate([cq0 + 256 + r(128), krope, krope]))
        per_head = DK + ROPE
        for i in range(6):
            if i < 4:
                cols = np.concatenate([(2 * i + e) * per_head + r(DK) for e in range(2)])
            else:
                cols = np.concatenate([(4 * (i - 4) + e) * per_head + DK + r(ROPE) for e in range(4)])
            p_ = blocks(w_uq[lyr], 0, KQ, cols)
            pieces.append(np.pad(p_, ((0, 0), (0, PIECE - p_.shape[1]))))
        for part in range(2):
            for half in range(2):
                cols = np.concatenate([(4 * half + e) * 2 * DK + part * DK + r(DK) for e in range(4)])
                pieces.append(blocks(w_ukv[lyr], 0, KKV, cols))
        for start, count in ((z0, 4), (g0, 8)):
            for i in range(count):
                wide(w_in[lyr], start + 256 * i + r(256))
        for w in (w_a, w_b, w_out):
            for i in range(4):
                wide(w[lyr], 256 * i + r(256))
        for i in range(16):
            wide(w_ff1[lyr], 256 * i + r(256))
        for i in range(4):
            wide(w_ff2[lyr], 256 * i + r(256), KF)
    return np.ascontiguousarray(np.stack(pieces))


def lay_out_params(p):
    out = []
    for lyr in range(DEPTH):
        cols = [p[n][lyr].reshape(-1, P).T for n in ("pre_mix_norm_w", "post_mix_norm_w", "pre_ffn_norm_w", "post_ffn_norm_w")]
        cols.append(p["conv_w"][lyr].reshape(-1, P).T)
        cols += [p[n][lyr].reshape(-1, P).T for n in ("q_a_norm_w", "kv_a_norm_w", "gdn_norm_w")]
        cols += [np.broadcast_to(p[n][lyr], (P, H)) for n in ("A_log", "dt_bias")]
        out.append(np.concatenate(cols, axis=1))
    return np.ascontiguousarray(np.stack(out, axis=1))


def kernel(**inputs):
    import concourse.bacc as _bacc
    from concourse.bass_utils import run_bass_kernel_spmd as _run

    a = {k: np.asarray(v) for k, v in inputs.items()}
    ab0 = QKV + H * DK
    arrays = {
        "x_t": np.ascontiguousarray(a["x"][0].T.reshape(KD, P, S).transpose(1, 0, 2)),
        "pos": np.ascontiguousarray(np.broadcast_to(a["positions"][0], (P, S))),
        "weights": lay_out_weights(a["w_in"], a["w_uq"], a["w_ukv"], a["w_branch_a"], a["w_branch_b"], a["w_out"],
                                   a["w_ff1"], a["w_ff2"]),
        "w_ab": np.ascontiguousarray(np.stack([blocks(a["w_in"][i], 0, KD, ab0 + np.arange(16)) for i in range(DEPTH)], axis=1)),
        "params": lay_out_params(a),
        "consts": constants(),
    }
    nc = _bacc.Bacc("TRN2", target_bir_lowering=False, num_devices=1)
    aps = [nc.dram_tensor(n, v.shape, mybir.dt.from_np(v.dtype), kind="ExternalInput").ap() for n, v in arrays.items()]
    out = nc.dram_tensor("out_t", (P, KD, S), F32, kind="ExternalOutput").ap()
    build(nc, *aps, out)
    r = _run(nc, [arrays], core_ids=[0])
    y = np.asarray(r.results[0]["out_t"])
    return np.ascontiguousarray(y.transpose(1, 0, 2).reshape(D, S).T)[None]
```

```python
from contextlib import ExitStack
import math

import numpy as np
import concourse.bass as bass
from concourse import mybir

F32 = mybir.dt.float32
F32R = mybir.dt.float32r
I32 = mybir.dt.int32
ALU = mybir.AluOpType
ACT = mybir.ActivationFunctionType
AX = mybir.AxisListType.X

P = 128
DEPTH, D, S = 2, 1024, 256
KD = D // P
NT = S // P
H, DK = 8, 128
ROPE, QL, KVL = 64, 384, 256
KQ, KKV = QL // P, KVL // P
EPS = 1e-6
CHUNK = 64
QKV = 3 * H * DK
FF = 4 * D
KF = FF // P
PIECE = 1024
PI_BELOW = 3.1415925
RING = 4
SIZES = [2 ** i for i in range(1, 7)]

PRE_MIX, POST_MIX, PRE_FFN, POST_FFN, CONV = 0, KD, 2 * KD, 3 * KD, 4 * KD
QA = CONV + 4 * (QKV // P)
KVA = QA + KQ
GDN = KVA + KKV
ALOG = GDN + 1
DTB = ALOG + H
NPRM = DTB + H

C_ID, C_UT, C_NEG, C_M1, C_LV, C_ONE, C_PERM, C_AM, C_FREQ = 0, 128, 256, 384, 512, 896, 1024, 1152, 1408
NCST = C_FREQ + 4


def jobs_of_a_layer():
    jobs, n = [], 0
    for kind, count, pieces in (("v", 4, 2), ("q", 4, 2), ("k", 4, 2), ("lat", 3, 2), ("kn", 4, 0.5), ("vt", 4, 0.5),
                                ("uq", 6, 1), ("z", 4, 2), ("gate", 8, 2), ("ya", 4, 2), ("yb", 4, 2),
                                ("out", 4, 2), ("ff1", 16, 2), ("ff2", 4, 8)):
        for i in range(count):
            jobs.append((kind, i, list(range(int(n), max(int(n) + 1, int(n + pieces))))))
            n += pieces
    return jobs, int(n)


JOBS, NPIECE = jobs_of_a_layer()
FIRST = {}
for _j, (_k, _i, _p) in enumerate(JOBS):
    FIRST.setdefault(_k, _j)
EVAC_BY_ACT = {"v", "q", "k", "uq", "kn", "vt", "z"}
NJOB = len(JOBS)
NACT_EVAC = sum(k in EVAC_BY_ACT for k, _, _ in JOBS)
NDVE_EVAC = NJOB - NACT_EVAC




def steps_through(n, job=False):
    if job:
        return sum(len(p) for _, _, p in JOBS[:n + 1])
    if n < 0:
        return n + 1
    return sum(len([q for q in p if q <= n]) for _, _, p in JOBS)


NSTEP = steps_through(NJOB - 1, job=True)


def evacs_through(j):
    mine = JOBS[j][0] in EVAC_BY_ACT
    return mine, sum((k in EVAC_BY_ACT) == mine for k, _, _ in JOBS[:j + 1])


def schedule():
    o = [("start", 0), ("sq", 0), ("sq", 1), ("sqsum", 0), ("sq", 2), ("sq", 3), ("sqsum", 1), ("norm", 0)]
    late = []

    def job(kind, i, after=None):
        o.append(("job", FIRST[kind] + i))
        flush()
        if after:
            late.append((after, i))

    def flush():
        o.extend(late)
        late.clear()

    for i in range(4):
        job("v", i)
        if i == 0:
            o.append(("ab", 0))
        o.append(("conv", i))
        if i == 1:
            o += [("logits", 0), ("silu", 0)]
        if i:
            late.append(("silu", i))
        if i == 3:
            o.append(("gc", 0))
    for i in range(4):
        job("q", i)
        o.append(("conv", 4 + i))
        late.append(("silu", 4 + i))
        if i:
            o += [("vtrans", i - 1), ("dt", i - 1)]
    for i in range(4):
        job("k", i)
        o.append(("conv", 8 + i))
        late.append(("silu", 8 + i))
        if i == 0:
            o += [("vtrans", 3), ("dt", 3)]
    job("lat", 0)
    o += [("lnexp", 0), ("nrm", 0), ("nrm", 1)]
    job("lat", 1)
    o += [("nrm", 2), ("latn", 0), ("nrm", 3)]
    job("lat", 2)
    o += [("nrm", 4), ("nrm", 5)]
    job("kn", 0)
    o += [("nrm", 6), ("nrm", 7)]
    job("kn", 1)
    o.append(("ktrans", 0))
    job("kn", 2)
    o += [("ktrans", 1), ("latn", 1)]
    job("kn", 3)
    for g in range(4):
        o.append(("decay", g))
        job("vt", g)
    for g in range(4):
        o.append(("x1", g))
        if g == 1:
            job("uq", 0)
    for lv in range(len(SIZES)):
        for step in ("lvP", "lvV", "lvT"):
            for g in range(4):
                o.append((step, lv * 4 + g))
            if step == "lvP" and lv < 5:
                job("uq", 1 + lv)
                if lv >= 3:
                    late.append(("qrope", lv - 3))
    flush()
    steps = ("t_v0", "t_st", "t_ks", "t_v1", "t_o")
    for n, step in enumerate(steps):
        o += [(step, 0), (step, 1)]
        if n < 4:
            job("z", n)
    o.append(("lnexp", 1))
    job("gate", 0)
    o += [("sc", 0), ("sc", 1), ("onrm", 0), ("onrm", 1)]
    job("gate", 1)
    o += [("onrm", 2), ("onrm", 3)]
    for n in range(6):
        job("gate", 2 + n)
        if n:
            o.append(("pv", n - 1))
        o.append(("tr", n))
        if n + 2 < 6:
            o.append(("sc", n + 2))
        if n < 2:
            o += [("osplit", 2 * n), ("osplit", 2 * n + 1)]
    o.append(("sig", 0))
    for i in range(4):
        job("ya", i)
        if i == 0:
            o.append(("pv", 5))
    for i in range(4):
        job("yb", i, "hsplit")
    flush()
    for i in range(4):
        job("out", i)
        if i in (1, 2):
            o.append(("yadd", i - 1))
    o += [("ysum", 0), ("post", 0), ("fsplit_x", 0)]
    for i in range(16):
        o.append(("job", FIRST["ff1"] + i))
        if i == 0:
            o.append(("squares", 1))
        if i == 1:
            o.append(("norm", 1))
        flush()
        late.append(("fsplit", i))
    flush()
    for i in range(4):
        job("ff2", i)
        if i in (1, 2):
            o.append(("yadd", 1 + i))
    o += [("ysum", 1), ("post", 1)]
    return o


ORDER = schedule()


def build(nc, x_in, pos_in, w_in, ab_in, prm_in, cst_in, out):
    with ExitStack() as ctx:
        base = [((nc.sbuf_base + 31) // 32) * 32]

        def at(name, shape, dtype, offset):
            return nc.alloc_sbuf_tensor_at(name, shape, dtype, offset=offset)

        def size(shape):
            return int(np.prod(shape[1:])) * 4

        def keep(name, shape, dtype=F32):
            t = at(name, shape, dtype, base[0])
            base[0] += (size(shape) + 31) // 32 * 32
            return t

        def psum(name):
            return ctx.enter_context(nc.psum_tensor(name, [P, 512], F32))

        xT = keep("xT", [P, KD, S])
        raw = [keep(f"raw{i}", [P, PIECE]) for i in range(RING)]
        whi = [keep(f"whi{i}", [P, PIECE], F32R) for i in range(RING)]
        wlo = [keep(f"wlo{i}", [P, PIECE], F32R) for i in range(RING)]
        cst = keep("cst", [P, NCST])
        prm_all = keep("prm_all", [P, DEPTH, NPRM])
        prm = keep("prm", [P, NPRM])
        cosT = keep("cosT", [P, S])
        sinT = keep("sinT", [P, S])
        sq = [keep(f"sq{i}", [P, 512]) for i in range(2)]
        rn = [keep(f"rn{i}", [P, 512]) for i in range(2)]
        ab_all = keep("ab_all", [P, DEPTH, KD * 16])
        ab_hi = keep("ab_hi", [P, KD * 16], F32R)
        ab_lo = keep("ab_lo", [P, KD * 16], F32R)
        sm = keep("sm", [P, 14, 32])
        gcT = keep("gcT", [8, S])
        mx = keep("mx", [P, 4])
        rs = keep("rs", [P, 4])
        bias_cols = keep("bias_cols", [P, 2])
        eps_col, lnscale_col = bias_cols[:, 0:1], bias_cols[:, 1:2]

        R0 = base[0]
        KIB = 1024

        def ph(name, shape, kib, dtype=F32):
            assert R0 + kib * KIB + size(shape) <= nc.sbuf_usable_end, name
            return at(name, shape, dtype, R0 + int(kib * KIB))

        uh = ph("uh", [P, KD, S], 0, F32R)
        ul = ph("ul", [P, KD, S], 8, F32R)
        qT = ph("qT", [P, H, S], 16)
        kT = ph("kT", [P, H, S], 24)
        vT = ph("vT", [P, H, S], 32)
        vtok = ph("vtok", [P, NT, H, DK], 40)
        ktok = ph("ktok", [P, H, DK], 48)
        DT = ph("DT", [P, 4, 4, P], 52)
        LT = ph("LT", [P, 4, 4, P], 60)
        XT = ph("XT", [P, 4, 4, P], 68)
        AT = ph("AT", [P, 4, 4, P], 76)
        cb = [ph(f"cb{i}", [P, 2, S], 99 + 2 * i) for i in range(2)]
        sq_kv = ph("sq_kv", [P, 2 * S], 76)
        sq_q = ph("sq_q", [P, 3 * S], 78)
        krx = ph("krx", [P, S], 81)
        kra = ph("kra", [P, S], 82)
        rl = ph("rl", [P, S], 83)
        latT = ph("latT", [P, 5, S], 84)
        lath = ph("lath", [P, 5, S], 89, F32R)
        latl = ph("latl", [P, 5, S], 94, F32R)
        qn = ph("qn", [P, H, S], 99)
        qr = ph("qr", [P, 4, S], 107)
        kn = ph("kn", [P, H, S], 111)
        kr = ph("kr", [P, S], 119)
        krz = ph("krz", [P, 2, S], 84)
        vt = ph("vt", [P, NT, H, DK], 120)
        utmp = ph("utmp", [P, KD, S], 99)
        usq = ph("usq", [P, KD, S], 107)
        abT = ph("abT", [16, S], 116)
        X = ph("X", [P, 4, 4, P], 52)
        PB = ph("PB", [P, 4, 4, 64], 32)
        qd = ph("qd", [P, H, P], 36)
        zs = ph("zs", [P, H, S], 16)
        vn0 = ph("vn0", [P, H, DK], 52)
        st = ph("st", [P, H, DK], 56)
        vn1 = ph("vn1", [P, H, DK], 60)
        rr = ph("rr", [P, H, DK], 64)
        oT = ph("oT", [P, H, S], 24)
        oh = ph("oh", [P, H, S], 91, F32R)
        ol = ph("ol", [P, H, S], 32, F32R)
        gates = ph("gates", [P, 2, KD, S], 40)
        E = [ph(f"E{i}", [P, 512], 60 + 2 * i) for i in range(2)]
        PT = [ph(f"PT{i}", [P, 512], 64 + 2 * i) for i in range(2)]
        ah = ph("ah", [P, H, S], 68, F32R)
        al = ph("al", [P, H, S], 76, F32R)
        hA = ph("hA", [P, KD, S], 16)
        hB = [ph(f"hB{i}", [P, 512], 24 + 2 * i) for i in range(2)]
        hh = ph("hh", [P, KD, S], 99, F32R)
        hl = ph("hl", [P, KD, S], 111, F32R)
        fuh = ph("fuh", [P, KD, S], 0, F32R)
        ful = ph("ful", [P, KD, S], 8, F32R)
        yT = ph("yT", [P, KD, S], 120)
        fusq = ph("fusq", [P, KD, S], 24)
        fh = ph("fh", [P, KF, S], 16, F32R)
        fl = ph("fl", [P, KF, S], 48, F32R)
        fr = [ph(f"fr{i}", [P, 512], 80 + 2 * i) for i in range(4)]
        pos_i = ph("pos_i", [P, S], 0, I32)
        ang = ph("ang", [P, 4, S], 8)

        dense = [psum(f"dense{i}") for i in range(3)]
        side = [psum(f"side{i}") for i in range(5)]

        ident = cst[:, C_ID:C_ID + P]
        upto = cst[:, C_UT:C_UT + P]
        future = cst[:, C_NEG:C_NEG + P]
        below1 = cst[:, C_M1:C_M1 + P]
        ones = cst[:, C_ONE:C_ONE + P]
        perm = cst[:, C_PERM:C_PERM + P]
        amask = cst[:, C_AM:C_AM + S]

        def over_heads(ap, n):
            return ap.rearrange("p (a w) -> p a w", a=1).broadcast_to([P, n, ap.shape[1]])

        def along(ap, w):
            return ap.rearrange("p (n a) -> p n a", a=1).broadcast_to([P, ap.shape[1], w])

        def S_(name):
            return ctx.enter_context(nc.semaphore(name))

        loaded = [S_(f"loaded{i}") for i in range(RING)]
        s_tab, s_x, s_in, s_out = S_("s_tab"), S_("s_x"), S_("s_in"), S_("s_out")
        s_trig, s_trig_a = S_("s_trig"), S_("s_trig_a")
        hi_ready, lo_ready, steps_done = S_("hi_ready"), S_("lo_ready"), S_("steps_done")
        act_evac, dve_evac = S_("act_evac"), S_("dve_evac")
        rises_per_layer = {}

        def signal(name, rises):
            s = S_(name)
            rises_per_layer[s.name] = rises
            return s

        fu_hi, fu_lo = (signal("fu_hi", 8), signal("fu_lo", 8))
        sq_sum_dve, sq_sum_pool = (signal("sq_sum_dve", 2), signal("sq_sum_pool", 2))
        x_by_pool, x_by_dve, y_add = (signal("x_by_pool", 4), signal("x_by_dve", 4), signal("y_add", 4))
        prm_ready, squared, sumsq, rnorm = (signal("prm_ready", 1), signal("squared", 8), signal("sumsq", 2), signal("rnorm", 4))
        pre_scaled, u_hi, u_lo, ab_split_hi = (signal("pre_scaled", 4), signal("u_hi", 4), signal("u_lo", 4), signal("ab_split_hi", 1))
        ab_t, ab_t_copied = (signal("ab_t", 1), signal("ab_t_copied", 1))
        ab_split_lo, ab_mm, ab_z, ab_abs = (signal("ab_split_lo", 1), signal("ab_mm", 1), signal("ab_z", 2), signal("ab_abs", 1))
        ab_ex, ab_w, ab_ln, ab_rc = (signal("ab_ex", 1), signal("ab_w", 2), signal("ab_ln", 1), signal("ab_rc", 1))
        ab_sp, ab_a, ab_g, gc_mm = (signal("ab_sp", 3), signal("ab_a", 2), signal("ab_g", 1), signal("gc_mm", 1))
        gc_copied, gc_exp, conv_mid, silu_done = (signal("gc_copied", 3), signal("gc_exp", 2), signal("conv_mid", 72), signal("silu_done", 12))
        tap0, dt_fut, dt_mm, dt_arg = (signal("tap0", 12), signal("dt_fut", 4), signal("dt_mm", 4), signal("dt_arg", 4))
        vtrans_mm, vtrans_out, nrm_sq, nrm_mm = (signal("vtrans_mm", 4), signal("vtrans_out", 4), signal("nrm_sq", 8), signal("nrm_mm", 8))
        nrm_r, nrm_out, lat_sq, lat_mm = (signal("nrm_r", 16), signal("nrm_out", 8), signal("lat_sq", 3), signal("lat_mm", 2))
        lat_r, lat_norm, lat_hi, lat_lo = (signal("lat_r", 4), signal("lat_norm", 2), signal("lat_hi", 2), signal("lat_lo", 2))
        kr_mm, kr_b, kr_out, ktrans_mm = (signal("kr_mm", 1), signal("kr_b", 3), signal("kr_out", 2), signal("ktrans_mm", 2))
        ktrans_out, dec_mm, dec_exp = (signal("ktrans_out", 2), signal("dec_mm", 4), signal("dec_exp", 4))
        dec_eg, dec_out, qd_out = (signal("dec_eg", 2), signal("dec_out", 8), signal("qd_out", 2))
        x1_mask, x1_xt, x1_mm, x1_out = (signal("x1_mask", 4), signal("x1_xt", 4), signal("x1_mm", 4), signal("x1_out", 4))
        lv_p, lv_p_out, lv_v = (signal("lv_p", 24), signal("lv_p_out", 24), signal("lv_v", 24))
        lv_x, lv_t, lv_t_out = (signal("lv_x", 24), signal("lv_t", 24), signal("lv_t_out", 24))
        t_v0m, t_v0o, t_stm, t_sto = (signal("t_v0m", 2), signal("t_v0o", 2), signal("t_stm", 2), signal("t_sto", 2))
        t_ksm, t_kst, t_kso, t_v1m = (signal("t_ksm", 2), signal("t_kst", 2), signal("t_kso", 2), signal("t_v1m", 2))
        t_v1o, t_om, t_oo, on_sq = (signal("t_v1o", 2), signal("t_om", 2), signal("t_oo", 2), signal("on_sq", 4))
        on_mm, on_r, on_o, on_z = (signal("on_mm", 4), signal("on_r", 8), signal("on_o", 4), signal("on_z", 4))
        on_hi, on_lo, qr_mm, qr_b = (signal("on_hi", 4), signal("on_lo", 4), signal("qr_mm", 2), signal("qr_b", 4))
        qr_out, sc_mm, sm_mask, sm_max = (signal("qr_out", 2), signal("sc_mm", 6), signal("sm_mask", 6), signal("sm_max", 6))
        sm_sub, sm_exp, sm_sum, sm_rec = (signal("sm_sub", 6), signal("sm_exp", 6), signal("sm_sum", 6), signal("sm_rec", 6))
        sm_out, tr_mm, tr_out, pv_mm = (signal("sm_out", 6), signal("tr_mm", 6), signal("tr_out", 6), signal("pv_mm", 6))
        pv_hi, pv_lo, sig_done, h_sum = (signal("pv_hi", 6), signal("pv_lo", 6), signal("sig_done", 4), signal("h_sum", 4))
        h_hi, h_lo, y_sq, y_mm = (signal("h_hi", 4), signal("h_lo", 4), signal("y_sq", 8), signal("y_mm", 2))
        y_r, y_scaled, f_sq = (signal("y_r", 4), signal("y_scaled", 8), signal("f_sq", 16))
        f_hi, f_lo = (signal("f_hi", 16), signal("f_lo", 16))

        block = ctx.enter_context(nc.Block())

        def due(l, s, n):
            return l * rises_per_layer[s.name] + n

        def products_done(l, j):
            return l * NSTEP + steps_through(j, job=True) + RING

        def unit(n):
            return (0, range(4 * n, 4 * n + 4)) if n < 2 else (1, range(2 * (n - 2), 2 * (n - 2) + 2))

        def conv_place(n):
            return [vT, qT, kT][n // 4], [2 * H, 0, H][n // 4] + 2 * (n % 4)

        def heads_of(g):
            return range(4 * (g % 2), 4 * (g % 2) + 4)

        def piece_width(n):
            kind = next(k for k, _, p in JOBS if n in p)
            return KQ * 256 if kind == "uq" else PIECE

        def splits_wanted(j):
            return NPIECE if j == NJOB - 1 else min(JOBS[j][2][-1] + RING, NPIECE)

        splits_at, seen = [], 0
        for what, n in ORDER:
            goal = splits_wanted(n) if what == "job" else 2 if (what, n) == ("norm", 0) else seen
            splits_at.append(range(seen, max(seen, goal)))
            seen = max(seen, goal)
        assert seen == NPIECE

        @block.sync
        def _(sp):
            sp.dma_start(pos_i[:], pos_in).then_inc(s_tab, 16)
            sp.dma_start(cst[:, C_FREQ:NCST], cst_in[:, C_FREQ:NCST]).then_inc(s_tab, 16)
            sp.dma_start(xT[:], x_in).then_inc(s_x, 16)
            sp.dma_start(prm_all[:], prm_in).then_inc(s_in, 16)
            sp.dma_start(cst[:, 0:C_FREQ], cst_in[:, 0:C_FREQ]).then_inc(s_in, 16)
            sp.dma_start(ab_all[:], ab_in).then_inc(s_in, 16)
            with sp.Fori(0, DEPTH * NPIECE // RING) as i:
                for s in range(RING):
                    sp.wait_ge(lo_ready, i * RING + s + 1)
                    sp.dma_start(raw[s][:], w_in[i * RING + s]).then_inc(loaded[s], 16)
            for c in range(4):
                pair = slice(2 * c, 2 * c + 2)
                x_pair = x_by_pool if c % 2 else x_by_dve
                sp.wait_ge(x_pair, due(DEPTH, x_pair, 1 + c // 2))
                sp.dma_start(out[:, pair, :], xT[:, pair, :]).then_inc(s_out, 16)
            sp.wait_ge(s_out, 4 * 16)

        @block.tensor
        def _(pe):
            mm = nc.tensor.matmul
            pe.sem_inc(steps_done, RING)

            def banks_free(l, j):
                if j >= 3:
                    by_act, n = evacs_through(j - 3)
                    if by_act:
                        pe.wait_ge(act_evac, l * NACT_EVAC + n)
                    else:
                        pe.wait_ge(dve_evac, l * NDVE_EVAC + n)

            def piece(l, n):
                pe.wait_ge(lo_ready, l * NPIECE + n + 1 + RING)
                return whi[n % RING], wlo[n % RING]

            def chunk_products(bank, n, k0, kcount, cols, ahi, alo, first, last, total_k, need=None):
                h_, l_ = whi[n % RING], wlo[n % RING]
                nch = cols // P
                for k in range(kcount):
                    if need is not None:
                        need(k0 + k)
                    for c in range(nch):
                        ws = slice(k * cols + c * P, k * cols + (c + 1) * P)
                        o_ = bank[:, c * S:(c + 1) * S]
                        is_first = first and k == 0 and c == 0
                        is_last = last and k == kcount - 1 and c == nch - 1
                        mm(o_, h_[:, ws], ahi[:, k0 + k, :], start=is_first, stop=False, skip_group_check=True)
                        mm(o_, h_[:, ws], alo[:, k0 + k, :], start=False, stop=False, skip_group_check=True)
                        x_ = mm(o_, l_[:, ws], ahi[:, k0 + k, :], start=False, stop=is_last, skip_group_check=True)
                return x_

            def job(l, j):
                kind, i, pieces = JOBS[j]
                bank = dense[j % 3]
                banks_free(l, j)
                if kind in ("v", "q", "k", "z", "gate", "lat"):
                    def need(k):
                        if kind == "v" and i == 0:
                            pe.wait_ge(u_lo, due(l, u_lo, k // 2 + 1))
                    for h_, n in enumerate(pieces):
                        piece(l, n)
                        r = chunk_products(bank, n, 4 * h_, 4, 256, uh, ul, h_ == 0, h_ == 1, KD, need)
                        r.then_inc(steps_done, 1)
                elif kind in ("ya", "yb", "out"):
                    a_, b_ = {"ya": (oh, ol), "yb": (ah, al), "out": (hh, hl)}[kind]
                    if kind == "yb" and i == 0:
                        pe.wait_ge(pv_lo, due(l, pv_lo, 6))

                    def need(k):
                        if kind == "ya" and i == 0:
                            pe.wait_ge(on_lo, due(l, on_lo, k // 2 + 1))
                        if kind == "out" and i == 0:
                            pe.wait_ge(h_lo, due(l, h_lo, k // 2 + 1))
                    for h_, n in enumerate(pieces):
                        piece(l, n)
                        r = chunk_products(bank, n, 4 * h_, 4, 256, a_, b_, h_ == 0, h_ == 1, KD, need)
                        r.then_inc(steps_done, 1)
                elif kind == "uq":
                    n = pieces[0]
                    piece(l, n)
                    if i == 0:
                        pe.wait_ge(lat_lo, due(l, lat_lo, 2))
                    r = chunk_products(bank, n, KKV, KQ, 256, lath, latl, True, True, KQ)
                    r.then_inc(steps_done, 1)
                elif kind == "kn":
                    n = pieces[0]
                    piece(l, n)
                    if i == 0:
                        pe.wait_ge(lat_lo, due(l, lat_lo, 1))
                    for c in range(2):
                        for k in range(KKV):
                            ws = slice(k * 512 + ((i % 2) * 2 + c) * P, k * 512 + ((i % 2) * 2 + c + 1) * P)
                            o_ = bank[:, c * S:(c + 1) * S]
                            mm(o_, whi[n % RING][:, ws], lath[:, k, :], start=(k == 0), stop=False)
                            mm(o_, whi[n % RING][:, ws], latl[:, k, :], start=False, stop=False)
                            r = mm(o_, wlo[n % RING][:, ws], lath[:, k, :], start=False, stop=(k == KKV - 1))
                    r.then_inc(steps_done, 1)
                elif kind == "vt":
                    n = pieces[0]
                    piece(l, n)
                    t = i % 2
                    for k in range(KKV):
                        a_, b_ = lath[:, k, t * P:(t + 1) * P], latl[:, k, t * P:(t + 1) * P]
                        ws = slice(k * 512, (k + 1) * 512)
                        mm(bank[:], a_, whi[n % RING][:, ws], start=(k == 0), stop=False)
                        mm(bank[:], a_, wlo[n % RING][:, ws], start=False, stop=False)
                        r = mm(bank[:], b_, whi[n % RING][:, ws], start=False, stop=(k == KKV - 1))
                    r.then_inc(steps_done, 1)
                elif kind == "ff1":
                    def need1(k):
                        if i == 0:
                            pe.wait_ge(fu_lo, due(l, fu_lo, k + 1))
                    for h_, n in enumerate(pieces):
                        piece(l, n)
                        r = chunk_products(bank, n, 4 * h_, 4, 256, fuh, ful, h_ == 0, h_ == 1, KD, need1)
                        r.then_inc(steps_done, 1)
                elif kind == "ff2":
                    for h_, n in enumerate(pieces):
                        piece(l, n)
                        if i == 0:
                            pe.wait_ge(f_lo, due(l, f_lo, 2 * h_ + 2))
                        r = chunk_products(bank, n, 4 * h_, 4, 256, fh, fl, h_ == 0, h_ == 7, KF)
                        r.then_inc(steps_done, 1)

            def norm(l, w):
                q_ = fusq if w else usq
                for c in (0, 1, 4, 5):
                    summed = sq_sum_pool if w else sq_sum_dve
                    if c % 4 == 0:
                        pe.wait_ge(summed, due(l, summed, c // 4 + 1))
                    r = mm(side[0][:, 0:S], ones, q_[:, c, :], start=(c == 0), stop=(c == 5))
                r.then_inc(sumsq, 1)

            def ab(l, _):
                pe.wait_ge(ab_split_lo, due(l, ab_split_lo, 1))
                pe.wait_ge(u_lo, due(l, u_lo, 4))
                for k in range(KD):
                    ws = slice(16 * k, 16 * k + 16)
                    o_ = side[1][0:16, 0:S]
                    mm(o_, ab_hi[:, ws], uh[:, k, :], start=(k == 0), stop=False)
                    mm(o_, ab_hi[:, ws], ul[:, k, :], start=False, stop=False)
                    r = mm(o_, ab_lo[:, ws], uh[:, k, :], start=False, stop=(k == KD - 1))
                r.then_inc(ab_t, 1)

            def logits(l, _):
                pe.wait_ge(ab_t_copied, due(l, ab_t_copied, 1))
                for t in range(NT):
                    r = mm(side[2][:, 16 * t:16 * t + 16], abT[:, t * P:(t + 1) * P], cst[0:16, C_ID:C_ID + 16],
                           start=True, stop=True)
                r.then_inc(ab_mm, 1)

            def gc(l, _):
                g_ = sm[:, 8, :].rearrange("p (t n) -> p t n", t=NT)
                pe.wait_ge(ab_g, due(l, ab_g, 1))
                pe.wait_ge(ab_a, due(l, ab_a, 2))
                mm(side[2][:, 0:32], upto, sm[:, 8, :], start=True, stop=True)
                mm(side[2][:, 32:64], ones, sm[:, 8, :], start=True, stop=True)
                for t in range(NT):
                    r = mm(side[2][0:8, 128 + t * P:128 + (t + 1) * P], g_[:, t, 0:8], upto, start=True, stop=True)
                r.then_inc(gc_mm, 1)

            def dt(l, g):
                pe.wait_ge(gc_copied, due(l, gc_copied, 3))
                if g == 3:
                    pe.wait_ge(dt_arg, due(l, dt_arg, 1))
                t = g // 2
                for e, h in enumerate(heads_of(g)):
                    one_row = cst[0:8, C_ID + h:C_ID + h + 1].broadcast_to([8, P])
                    r = mm(side[g % 3][:, e * P:(e + 1) * P], one_row, gcT[:, t * P:(t + 1) * P], start=True, stop=True)
                r.then_inc(dt_mm, 1)

            def vtrans(l, i):
                t, half = i // 2, i % 2
                if i == 0:
                    pe.wait_ge(silu_done, due(l, silu_done, 4))
                if i >= 2:
                    pe.wait_ge(vtrans_out, due(l, vtrans_out, i - 1))
                for e in range(4):
                    r = nc.tensor.transpose(side[3 + i % 2][:, e * P:(e + 1) * P],
                                            vT[:, 4 * half + e, t * P:(t + 1) * P], ident)
                r.then_inc(vtrans_mm, 1)

            def nrm(l, i):
                pe.wait_ge(nrm_sq, due(l, nrm_sq, i + 1))
                if i == 0:
                    pe.wait_ge(dt_arg, due(l, dt_arg, 2))
                    pe.wait_ge(vtrans_out, due(l, vtrans_out, 3))
                if i >= 2:
                    pe.wait_ge(nrm_r, due(l, nrm_r, 2 * (i - 2) + 1))
                mm(side[1 + 2 * (i % 2)][:], ones, sq[i % 2][:], start=True, stop=True).then_inc(nrm_mm, 1)

            def latn(l, i):
                if i == 0:
                    pe.wait_ge(vtrans_out, due(l, vtrans_out, 4))
                    pe.wait_ge(lat_sq, due(l, lat_sq, 1))
                    for e in range(2):
                        r = mm(side[4][:, 0:S], ones, sq_kv[:, e * S:(e + 1) * S], start=(e == 0), stop=(e == 1))
                    r.then_inc(lat_mm, 1)
                else:
                    pe.wait_ge(lat_r, due(l, lat_r, 1))
                    pe.wait_ge(dve_evac, l * NDVE_EVAC + evacs_through(FIRST["lat"] + 2)[1])
                    mm(side[4][:, S:2 * S], perm, krx[:], start=True, stop=True).then_inc(kr_mm, 1)
                    pe.wait_ge(lat_sq, due(l, lat_sq, 3))
                    for e in range(3):
                        r = mm(side[4][:, 0:S], ones, sq_q[:, e * S:(e + 1) * S], start=(e == 0), stop=(e == 2))
                    r.then_inc(lat_mm, 1)

            def ktrans(l, half):
                pe.wait_ge(nrm_out, due(l, nrm_out, 6 + 2 * half))
                if half == 0:
                    pe.wait_ge(dec_eg, due(l, dec_eg, 1))
                for e in range(4):
                    r = nc.tensor.transpose(side[2 + half][:, e * P:(e + 1) * P], kT[:, 4 * half + e, 0:P], ident)
                r.then_inc(ktrans_mm, 1)

            def decay(l, g):
                b_ = 2 * (g % 2)
                if g == 0:
                    pe.wait_ge(nrm_out, due(l, nrm_out, 8))
                    pe.wait_ge(dec_eg, due(l, dec_eg, 2))
                elif g == 1:
                    pe.wait_ge(ktrans_out, due(l, ktrans_out, 2))
                else:
                    pe.wait_ge(dec_out, due(l, dec_out, 2 * (g - 1)))
                for e, h in enumerate(heads_of(g)):
                    cols = slice(e * P, (e + 1) * P)
                    ts_ = slice(g // 2 * P, (g // 2 + 1) * P)
                    mm(side[b_][:, cols], kT[:, h, ts_], kT[:, h, ts_], start=True, stop=True)
                    r = mm(side[b_ + 1][:, cols], kT[:, h, ts_], qT[:, h, ts_], start=True, stop=True)
                r.then_inc(dec_mm, 1)

            def x1(l, g):
                pe.wait_ge(x1_xt, due(l, x1_xt, g + 1))
                pe.wait_ge(dec_out, due(l, dec_out, 8))
                for e in range(4):
                    r = nc.tensor.transpose(side[g][:, e * P:(e + 1) * P], XT[:, g, e, :], ident)
                r.then_inc(x1_mm, 1)

            def evens(ap, s):
                return ap.rearrange("p (b two s) -> p b two s", two=2, s=s)[:, :, 0, :]

            def lvP(l, i):
                lv, g = divmod(i, 4)
                s = SIZES[lv]
                if lv == 0:
                    pe.wait_ge(x1_out, due(l, x1_out, g + 1))
                else:
                    pe.wait_ge(lv_t_out, due(l, lv_t_out, i - 3))
                for e in range(4):
                    r = mm(side[g][:, e * 64:(e + 1) * 64], LT[:, g, e, :], evens(X[:, g, e, :], s), start=True, stop=True)
                r.then_inc(lv_p, 1)

            def lvV(l, i):
                g = i % 4
                pe.wait_ge(lv_p_out, due(l, lv_p_out, i + 1))
                for e in range(4):
                    r = mm(side[g][:, e * 64:(e + 1) * 64], XT[:, g, e, :], PB[:, g, e, :], start=True, stop=True)
                r.then_inc(lv_v, 1)

            def lvT(l, i):
                g = i % 4
                pe.wait_ge(lv_x, due(l, lv_x, i + 1))
                for e in range(4):
                    r = nc.tensor.transpose(side[g][:, e * P:(e + 1) * P], X[:, g, e, :], ident)
                r.then_inc(lv_t, 1)

            def t_v0(l, half):
                pe.wait_ge(lv_t_out, due(l, lv_t_out, 20 + half + 1))
                for e in range(4):
                    r = mm(side[half][:, e * P:(e + 1) * P], XT[:, half, e, :], vtok[:, 0, 4 * half + e, :],
                           start=True, stop=True)
                r.then_inc(t_v0m, 1)

            def t_st(l, half):
                pe.wait_ge(t_v0o, due(l, t_v0o, half + 1))
                pe.wait_ge(lv_t_out, due(l, lv_t_out, 22 + half + 1))
                for e in range(4):
                    h = 4 * half + e
                    r = mm(side[2 + half][:, e * P:(e + 1) * P], ktok[:, h, :], vn0[:, h, :], start=True, stop=True)
                r.then_inc(t_stm, 1)

            def t_ks(l, half):
                pe.wait_ge(t_sto, due(l, t_sto, half + 1))
                for e in range(4):
                    h = 4 * half + e
                    r = mm(side[half][:, e * P:(e + 1) * P], kT[:, h, P:2 * P], st[:, h, :], start=True, stop=True)
                r.then_inc(t_ksm, 1)

            def t_v1(l, half):
                pe.wait_ge(t_kso, due(l, t_kso, half + 1))
                for e in range(4):
                    h = 4 * half + e
                    r = mm(side[2 + half][:, e * P:(e + 1) * P], XT[:, 2 + half, e, :], rr[:, h, :], start=True, stop=True)
                r.then_inc(t_v1m, 1)

            def t_o(l, half):
                pe.wait_ge(t_v1o, due(l, t_v1o, half + 1))
                pe.wait_ge(qd_out, due(l, qd_out, 2))
                for e in range(4):
                    h = 4 * half + e
                    cols = slice(e * P, (e + 1) * P)
                    mm(side[half][:, cols], vn0[:, h, :], AT[:, half, e, :], start=True, stop=True)
                    mm(side[2 + half][:, cols], st[:, h, :], qd[:, h, :], start=True, stop=False)
                    r = mm(side[2 + half][:, cols], vn1[:, h, :], AT[:, 2 + half, e, :], start=False, stop=True)
                r.then_inc(t_om, 1)

            def onrm(l, i):
                pe.wait_ge(on_sq, due(l, on_sq, i + 1))
                if i < 2:
                    pe.wait_ge(t_oo, due(l, t_oo, 2))
                else:
                    pe.wait_ge(on_r, due(l, on_r, 2 * (i - 2) + 1))
                mm(side[3 + i % 2][:], ones, sq[i % 2][:], start=True, stop=True).then_inc(on_mm, 1)

            def qrope(l, i):
                if i == 0:
                    pe.wait_ge(kr_out, due(l, kr_out, 2))
                else:
                    pe.wait_ge(qr_b, due(l, qr_b, 2 * i - 1))
                pe.wait_ge(act_evac, l * NACT_EVAC + evacs_through(FIRST["uq"] + 4 + i)[1])
                mm(side[4][:], perm, qr[:, 2 * i:2 * i + 2, :], start=True, stop=True).then_inc(qr_mm, 1)

            def sc(l, n):
                qt, hs = unit(n)
                w = P * (qt + 1)
                if n == 0:
                    pe.wait_ge(t_oo, due(l, t_oo, 2))
                    pe.wait_ge(kr_out, due(l, kr_out, 2))
                    pe.wait_ge(qr_out, due(l, qr_out, 2))
                    pe.wait_ge(act_evac, l * NACT_EVAC + evacs_through(FIRST["vt"] + 3)[1])
                elif n >= 2:
                    pe.wait_ge(sm_mask, due(l, sm_mask, n - 1))
                for e, h in enumerate(hs):
                    o_ = side[n % 2][:, e * w:(e + 1) * w]
                    mm(o_, qn[:, h, qt * P:(qt + 1) * P], kn[:, h, 0:w], start=True, stop=False)
                    r = mm(o_, qr[:, h // 2, qt * P:(qt + 1) * P], krz[:, h % 2, 0:w],
                           start=False, stop=True)
                r.then_inc(sc_mm, 1)

            def tr(l, n):
                pe.wait_ge(sm_out, due(l, sm_out, n + 1))
                if n >= 1:
                    pe.wait_ge(tr_out, due(l, tr_out, n))
                for e in range(4):
                    r = nc.tensor.transpose(side[2][:, e * P:(e + 1) * P], E[n % 2][:, e * P:(e + 1) * P], ident)
                r.then_inc(tr_mm, 1)

            def pv(l, n):
                qt, hs = unit(n)
                pe.wait_ge(tr_out, due(l, tr_out, n + 1))
                if n >= 2:
                    pe.wait_ge(pv_lo, due(l, pv_lo, n - 1))
                else:
                    pe.wait_ge(on_r, due(l, on_r, 8))
                for e, h in enumerate(hs):
                    o_ = side[3 + n % 2][:, e * P:(e + 1) * P]
                    for kt in range(qt + 1):
                        p_ = PT[n % 2][:, (e * (qt + 1) + kt) * P:(e * (qt + 1) + kt + 1) * P]
                        r = mm(o_, vt[:, kt, h, :], p_, start=(kt == 0), stop=(kt == qt))
                r.then_inc(pv_mm, 1)

            def ysum(l, w):
                pe.wait_ge(y_add, due(l, y_add, 2 * w + 2))
                for n in range(2):
                    if n:
                        pe.wait_ge(y_sq, due(l, y_sq, 4 * w + 4))
                    for e in range(2):
                        r = mm(side[1][:, 0:S], ones, sq[n][:, e * S:(e + 1) * S], start=(n == 0 and e == 0),
                               stop=(n == 1 and e == 1))
                r.then_inc(y_mm, 1)

            do = dict(norm=norm, ab=ab, logits=logits, dt=dt, job=job, gc=gc, vtrans=vtrans, nrm=nrm, latn=latn, ktrans=ktrans, decay=decay, x1=x1,
                      lvP=lvP, lvV=lvV, lvT=lvT, t_v0=t_v0, t_st=t_st, t_ks=t_ks, t_v1=t_v1, t_o=t_o, onrm=onrm,
                      sc=sc, tr=tr, pv=pv, ysum=ysum, qrope=qrope)
            pe.wait_ge(s_in, 3 * 16)
            with pe.Fori(0, DEPTH) as l:
                for what, n in ORDER:
                    if what in do:
                        do[what](l, n)

        @block.scalar
        def _(act):
            A = nc.scalar.activation

            def copy(o_, i_):
                return A(o_, i_, ACT.Copy)

            def split_hi(l, n):
                s = n % RING
                w = piece_width(n)
                act.wait_ge(loaded[s], (l * (NPIECE // RING) + n // RING + 1) * 16)
                act.wait_ge(steps_done, l * NSTEP + steps_through(n - RING) + RING)
                copy(whi[s][:, 0:w], raw[s][:, 0:w]).then_inc(hi_ready, 1)

            def rsqrt(l, rises, n, out_, in_, scale, bias_exp):
                A(out_, in_, ACT.Ln, scale=scale, bias=eps_col).then_inc(rises, 1)
                act.wait_ge(rises, due(l, rises, 2 * n + 1))
                A(out_, out_, ACT.Exp, scale=-0.5, bias=bias_exp).then_inc(rises, 1)

            def sq_(l, n):
                w, c = divmod(n, 4)
                pair = slice(2 * c, 2 * c + 2)
                x_pair = x_by_pool if c % 2 else x_by_dve
                act.wait_ge(x_pair, due(l, x_pair, 1 + 2 * w + c // 2))
                A((fusq if w else usq)[:, pair, :], xT[:, pair, :], ACT.Square).then_inc(squared, 1)

            def squares(l, _):
                for n in range(4, 8):
                    sq_(l, n)

            def norm(l, w):
                act.wait_ge(sumsq, due(l, sumsq, w + 1))
                rsqrt(l, rnorm, w, rn[1][:, 0:S], side[0][:, 0:S], 1.0 / D, 0.0)
                if w == 0:
                    for c in range(4):
                        pair = slice(2 * c, 2 * c + 2)
                        act.wait_ge(pre_scaled, due(l, pre_scaled, c + 1))
                        copy(uh[:, pair, :], utmp[:, pair, :]).then_inc(u_hi, 1)
                if w == 0:
                    act.wait_ge(prm_ready, due(l, prm_ready, 1))
                    copy(ab_hi[:], ab_all[:, l, :]).then_inc(ab_split_hi, 1)
                    A(sm[:, 12, 0:H], prm[:, ALOG:ALOG + H], ACT.Exp).then_inc(ab_a, 1)

            def fsplit_x(l, _):
                for c in range(KD):
                    x_pair = x_by_pool if c // 2 % 2 else x_by_dve
                    if c % 2 == 0:
                        act.wait_ge(x_pair, due(l, x_pair, 3 + c // 4))
                    A(fuh[:, c, :], xT[:, c, :], ACT.Identity,
                      scale=prm[:, PRE_FFN + c:PRE_FFN + c + 1]).then_inc(fu_hi, 1)

            def logits(l, _):
                act.wait_ge(ab_z, due(l, ab_z, 2))
                A(sm[:, 1, :], sm[:, 0, :], ACT.Abs).then_inc(ab_abs, 1)
                act.wait_ge(ab_abs, due(l, ab_abs, 1))
                A(sm[:, 2, :], sm[:, 1, :], ACT.Exp, scale=-1.0).then_inc(ab_ex, 1)
                act.wait_ge(ab_w, due(l, ab_w, 1))
                A(sm[:, 4, :], sm[:, 3, :], ACT.Ln).then_inc(ab_ln, 1)
                act.wait_ge(ab_sp, due(l, ab_sp, 3))
                A(sm[:, 8, :].rearrange("p (t n) -> p t n", t=NT)[:, :, 8:16],
                  sm[:, 7, :].rearrange("p (t n) -> p t n", t=NT)[:, :, 8:16], ACT.Exp, scale=-1.0).then_inc(ab_a, 1)

            def job(l, j):
                kind, i, _ = JOBS[j]
                bank = dense[j % 3]
                if kind not in EVAC_BY_ACT and kind not in ("lat", "out", "ff2"):
                    return
                act.wait_ge(steps_done, products_done(l, j))
                pair = slice(2 * i, 2 * i + 2)
                if kind in ("v", "q", "k"):
                    n = j
                    dst, chunk0 = conv_place(n)
                    for c in range(2):
                        x_ = A(dst[:, 2 * (n % 4) + c, :], bank[:, c * S:(c + 1) * S], ACT.Identity,
                               scale=prm[:, CONV + 3 * (QKV // P) + chunk0 + c:CONV + 3 * (QKV // P) + chunk0 + c + 1])
                    x_.then_inc(tap0, 1)
                    if n >= 2:
                        act.wait_ge(conv_mid, due(l, conv_mid, 6 * (n - 1)))
                    copy(cb[n % 2][:], bank[:]).then_inc(act_evac, 1)
                elif kind == "lat":
                    if i < 2:
                        A(sq_kv[:] if i == 0 else sq_q[:, 0:512], bank[:], ACT.Square).then_inc(lat_sq, 1)
                    else:
                        A(sq_q[:, 512:768], bank[:, 0:S], ACT.Square).then_inc(lat_sq, 1)
                elif kind == "uq":
                    dst = qn[:, pair, :] if i < 4 else qr[:, 2 * (i - 4):2 * (i - 4) + 2, :]
                    copy(dst, bank[:]).then_inc(act_evac, 1)
                elif kind == "kn":
                    copy(kn[:, pair, :], bank[:]).then_inc(act_evac, 1)
                elif kind == "vt":
                    h0 = 4 * (i // 2)
                    copy(vt[:, i % 2, h0:h0 + 4, :], bank[:]).then_inc(act_evac, 1)
                elif kind == "z":
                    if i == 0:
                        act.wait_ge(qd_out, due(l, qd_out, 2))
                    A(zs[:, pair, :], bank[:], ACT.Silu).then_inc(act_evac, 1)
                elif kind in ("out", "ff2"):
                    w = kind == "ff2"
                    if i >= 2:
                        act.wait_ge(y_add, due(l, y_add, 2 * w + i - 1))
                    A(sq[min(i, 1)][:], bank[:], ACT.Square).then_inc(y_sq, 1)

            def silu(l, n):
                dst = conv_place(n)[0][:, 2 * (n % 4):2 * (n % 4) + 2, :]
                act.wait_ge(conv_mid, due(l, conv_mid, 6 * (n + 1)))
                A(dst, dst, ACT.Silu).then_inc(silu_done, 1)

            def vtrans(l, i):
                t, half = i // 2, i % 2
                act.wait_ge(vtrans_mm, due(l, vtrans_mm, i + 1))
                copy(vtok[:, t, 4 * half:4 * half + 4, :], side[3 + i % 2][:]).then_inc(vtrans_out, 1)

            def lnexp(l, i):
                nc.scalar.preload_act_table_set("natural_log_exp_and_others")
                if i == 0:
                    act.wait_ge(gc_copied, due(l, gc_copied, 3))
                    A(sm[:, 11, :], sm[:, 9, :], ACT.Exp).then_inc(gc_exp, 1)
                    A(sm[:, 13, :], sm[:, 10, :], ACT.Exp).then_inc(gc_exp, 1)

            def nrm(l, i):
                act.wait_ge(nrm_mm, due(l, nrm_mm, i + 1))
                if i >= 2:
                    act.wait_ge(nrm_out, due(l, nrm_out, i - 1))
                rsqrt(l, nrm_r, i, rn[i % 2][:], side[1 + 2 * (i % 2)][:], 1.0, lnscale_col if i < 4 else 0.0)
                if i in (2, 3):
                    act.wait_ge(vtrans_mm, due(l, vtrans_mm, 4))
                    act.wait_ge(dt_arg, due(l, dt_arg, i + 1))
                    A(qd[:, 4 * (i - 2):4 * (i - 1), :], side[2 if i == 2 else 0][:], ACT.Exp).then_inc(dec_eg, 1)

            def decay(l, g):
                act.wait_ge(dt_arg, due(l, dt_arg, g + 1))
                A(DT[:, g], DT[:, g], ACT.Exp).then_inc(dec_exp, 1)

            def latn(l, n):
                act.wait_ge(lat_mm, due(l, lat_mm, n + 1))
                if n:
                    act.wait_ge(lat_norm, due(l, lat_norm, 1))
                rsqrt(l, lat_r, n, rl[:], side[4][:, 0:S], 1.0 / (QL if n else KVL), 0.0)
                a_, b_ = (2, 5) if n else (0, 2)
                act.wait_ge(lat_norm, due(l, lat_norm, n + 1))
                copy(lath[:, a_:b_, :], latT[:, a_:b_, :]).then_inc(lat_hi, 1)

            def x1(l, g):
                act.wait_ge(x1_mm, due(l, x1_mm, g + 1))
                copy(X[:, g], side[g][:]).then_inc(x1_out, 1)

            def lvT(l, i):
                act.wait_ge(lv_t, due(l, lv_t, i + 1))
                copy(XT[:, i % 4], side[i % 4][:]).then_inc(lv_t_out, 1)

            def t_st(l, half):
                act.wait_ge(t_stm, due(l, t_stm, half + 1))
                copy(st[:, 4 * half:4 * half + 4, :], side[2 + half][:]).then_inc(t_sto, 1)

            def t_o(l, half):
                hs = slice(4 * half, 4 * half + 4)
                act.wait_ge(t_om, due(l, t_om, half + 1))
                copy(oT[:, hs, 0:P], side[half][:])
                copy(oT[:, hs, P:2 * P], side[2 + half][:]).then_inc(t_oo, 1)

            def onrm(l, i):
                act.wait_ge(on_mm, due(l, on_mm, i + 1))
                if i >= 2:
                    act.wait_ge(on_o, due(l, on_o, i - 1))
                rsqrt(l, on_r, i, rn[i % 2][:], side[3 + i % 2][:], 1.0 / DK, 0.0)

            def osplit(l, i):
                act.wait_ge(on_z, due(l, on_z, i + 1))
                copy(oh[:, 2 * i:2 * i + 2, :], oT[:, 2 * i:2 * i + 2, :]).then_inc(on_hi, 1)

            def sc(l, n):
                act.wait_ge(sm_sub, due(l, sm_sub, n + 1))
                A(E[n % 2][:], E[n % 2][:], ACT.Exp, scale=float((DK + ROPE) ** -0.5)).then_inc(sm_exp, 1)

            def tr(l, n):
                act.wait_ge(tr_mm, due(l, tr_mm, n + 1))
                if n >= 2:
                    act.wait_ge(pv_mm, due(l, pv_mm, n - 1))
                copy(PT[n % 2][:], side[2][:]).then_inc(tr_out, 1)

            def pv(l, n):
                qt, hs = unit(n)
                nh = len(hs)
                act.wait_ge(pv_mm, due(l, pv_mm, n + 1))
                copy(ah[:, hs[0]:hs[0] + nh, qt * P:(qt + 1) * P], side[3 + n % 2][:, 0:nh * P]).then_inc(pv_hi, 1)

            def sig(l, _):
                nc.scalar.preload_act_table(ACT.Sigmoid)
                act.wait_ge(dve_evac, l * NDVE_EVAC + evacs_through(FIRST["gate"] + 7)[1])
                flat = gates[:].rearrange("p b c s -> p (b c s)")
                for i in range(4):
                    part = flat[:, i * 1024:(i + 1) * 1024]
                    A(part, part, ACT.Sigmoid).then_inc(sig_done, 1)
                nc.scalar.preload_act_table_set("natural_log_exp_and_others")

            def hsplit(l, i):
                act.wait_ge(h_sum, due(l, h_sum, i + 1))
                copy(hh[:, 2 * i:2 * i + 2, :], hA[:, 2 * i:2 * i + 2, :]).then_inc(h_hi, 1)

            def post(l, w):
                act.wait_ge(y_mm, due(l, y_mm, w + 1))
                rsqrt(l, y_r, w, rn[0][:, 0:S], side[1][:, 0:S], 1.0 / D, 0.0)

            def fsplit(l, i):
                act.wait_ge(f_sq, due(l, f_sq, i + 1))
                copy(fh[:, 2 * i:2 * i + 2, :], fr[i % 4][:]).then_inc(f_hi, 1)

            do = dict(sq=sq_, squares=squares, norm=norm, fsplit_x=fsplit_x, logits=logits, job=job, silu=silu, vtrans=vtrans, lnexp=lnexp, nrm=nrm, latn=latn,
                      decay=decay, x1=x1, lvT=lvT, t_st=t_st, t_o=t_o, onrm=onrm, osplit=osplit, sc=sc, tr=tr, pv=pv, sig=sig,
                      hsplit=hsplit, post=post, fsplit=fsplit)
            act.wait_ge(s_trig, 12)
            A(cosT[:], ang[:, 0, :], ACT.Sin).then_inc(s_trig_a, 1)
            act.wait_ge(s_trig, 20)
            A(sinT[:], ang[:, 1, :], ACT.Sin).then_inc(s_trig_a, 1)
            act.wait_ge(s_x, 16)
            nc.scalar.preload_act_table_set("natural_log_exp_and_others")
            with act.Fori(0, DEPTH) as l:
                for (what, n), pieces in zip(ORDER, splits_at):
                    for p_ in pieces:
                        split_hi(l, p_)
                    if what in do:
                        do[what](l, n)

        @block.vector
        def _(dve):
            V = nc.vector
            TT, TS, STT = V.tensor_tensor, V.tensor_scalar, V.scalar_tensor_tensor
            dve.sem_inc(lo_ready, RING)
            dve.sem_inc(x_by_dve, 2)

            def f32(ap):
                return ap.bitcast(F32)

            def split_lo(l, n):
                s = n % RING
                w = piece_width(n)
                dve.wait_ge(hi_ready, l * NPIECE + n + 1)
                TT(wlo[s][:, 0:w], raw[s][:, 0:w], f32(whi[s][:, 0:w]), ALU.subtract).then_inc(lo_ready, 1)

            def col(n):
                return prm[:, n:n + 1]

            def start(l, _):
                V.tensor_copy(prm[:], prm_all[:, l, :]).then_inc(prm_ready, 1)

            def sqsum(l, n):
                c = 4 * n
                dve.wait_ge(squared, due(l, squared, 2 * n + 2))
                TT(usq[:, c:c + 2, :], usq[:, c:c + 2, :], usq[:, c + 2:c + 4, :], ALU.add).then_inc(sq_sum_dve, 1)

            def norm(l, w):
                if w:
                    return
                dve.wait_ge(prm_ready, due(l, prm_ready, 1))
                dve.wait_ge(x_by_pool, due(l, x_by_pool, 2))
                dve.wait_ge(x_by_dve, due(l, x_by_dve, 2))
                dve.wait_ge(rnorm, due(l, rnorm, 2))

                def low(c):
                    pair = slice(2 * c, 2 * c + 2)
                    dve.wait_ge(u_hi, due(l, u_hi, c + 1))
                    TT(ul[:, pair, :], utmp[:, pair, :], f32(uh[:, pair, :]), ALU.subtract).then_inc(u_lo, 1)

                for c in range(4):
                    for e in (2 * c, 2 * c + 1):
                        x_ = STT(utmp[:, e, :], xT[:, e, :], col(PRE_MIX + e), rn[1][:, 0:S], ALU.mult, ALU.mult)
                    x_.then_inc(pre_scaled, 1)
                    if c >= 1:
                        low(c - 1)
                low(3)
                dve.wait_ge(ab_split_hi, due(l, ab_split_hi, 1))
                TT(ab_lo[:], ab_all[:, l, :], f32(ab_hi[:]), ALU.subtract).then_inc(ab_split_lo, 1)

            def ab(l, _):
                dve.wait_ge(ab_t, due(l, ab_t, 1))
                V.tensor_copy(abT[:], side[1][0:16, 0:S]).then_inc(ab_t_copied, 1)

            def logits(l, _):
                by_t = lambda n: sm[:, n, :].rearrange("p (t n) -> p t n", t=NT)
                over_t = lambda ap: ap.rearrange("p (a n) -> p a n", a=1).broadcast_to([P, NT, H])
                dve.wait_ge(ab_mm, due(l, ab_mm, 1))
                raw_ = side[2][:, 0:32].rearrange("p (t n) -> p t n", t=NT)
                TT(by_t(0)[:, :, 0:8], raw_[:, :, 0:8], over_t(prm[:, DTB:DTB + H]), ALU.add).then_inc(ab_z, 1)
                TS(by_t(0)[:, :, 8:16], raw_[:, :, 8:16], -1.0, None, ALU.mult).then_inc(ab_z, 1)
                dve.wait_ge(ab_ex, due(l, ab_ex, 1))
                TS(sm[:, 3, :], sm[:, 2, :], 1.0, None, ALU.add).then_inc(ab_w, 1)
                dve.wait_ge(ab_w, due(l, ab_w, 1))
                STT(sm[:, 5, :], sm[:, 3, :], -1.0, sm[:, 2, :], ALU.add, ALU.subtract).then_inc(ab_w, 1)
                V.reciprocal(sm[:, 6, :], sm[:, 3, :]).then_inc(ab_rc, 1)
                dve.wait_ge(ab_w, due(l, ab_w, 2))
                dve.wait_ge(ab_rc, due(l, ab_rc, 1))
                TT(sm[:, 5, :], sm[:, 5, :], sm[:, 6, :], ALU.mult).then_inc(ab_sp, 1)
                dve.wait_ge(ab_sp, due(l, ab_sp, 1))
                dve.wait_ge(ab_ln, due(l, ab_ln, 1))
                TT(sm[:, 7, :], sm[:, 4, :], sm[:, 5, :], ALU.subtract).then_inc(ab_sp, 1)
                dve.wait_ge(ab_sp, due(l, ab_sp, 2))
                STT(sm[:, 7, :], sm[:, 0, :], 0.0, sm[:, 7, :], ALU.max, ALU.add).then_inc(ab_sp, 1)
                dve.wait_ge(ab_sp, due(l, ab_sp, 3))
                dve.wait_ge(ab_a, due(l, ab_a, 1))
                STT(by_t(8)[:, :, 0:8], by_t(7)[:, :, 0:8], -1.0, over_t(sm[:, 12, 0:H]), ALU.mult,
                    ALU.mult).then_inc(ab_g, 1)

            def gc(l, _):
                dve.wait_ge(gc_mm, due(l, gc_mm, 1))
                V.tensor_copy(sm[:, 9, :], side[2][:, 0:32]).then_inc(gc_copied, 1)
                V.tensor_copy(gcT[:], side[2][0:8, 128:384]).then_inc(gc_copied, 1)
                dve.wait_ge(gc_copied, due(l, gc_copied, 1))
                TT(sm[:, 10, :], side[2][:, 32:64], sm[:, 9, :], ALU.subtract).then_inc(gc_copied, 1)

            def conv(l, n):
                dst, chunk0 = conv_place(n)
                dve.wait_ge(tap0, due(l, tap0, n + 1))
                dve.wait_ge(act_evac, l * NACT_EVAC + n + 1)
                for back in range(1, 4):
                    for c in range(2):
                        m = 2 * (back - 1) + c
                        y_, x_ = dst[:, 2 * (n % 4) + c, back:], cb[n % 2][:, c, 0:S - back]
                        if back > 1:
                            dve.wait_ge(conv_mid, due(l, conv_mid, 6 * n + m - 1))
                        STT(y_, x_, col(CONV + (3 - back) * (QKV // P) + chunk0 + c), y_, ALU.mult,
                            ALU.add).then_inc(conv_mid, 1)

            def dt(l, g):
                dve.wait_ge(dt_mm, due(l, dt_mm, g + 1))
                dve.wait_ge(dt_fut, due(l, dt_fut, g + 1))
                TT(DT[:, g], heads4(side[g % 3][:]), DT[:, g], ALU.add).then_inc(dt_arg, 1)

            def nrm(l, i):
                dst = [qT, kT][i // 4][:, 2 * (i % 4):2 * (i % 4) + 2, :]
                dve.wait_ge(nrm_r, due(l, nrm_r, 2 * i + 2))
                TT(dst, dst, rn[i % 2][:].rearrange("p (c s) -> p c s", c=2), ALU.mult).then_inc(nrm_out, 1)

            def latn(l, n):
                a_, b_ = (2, 5) if n else (0, 2)
                dve.wait_ge(lat_r, due(l, lat_r, 2 * n + 2))
                dve.wait_ge(dve_evac, l * NDVE_EVAC + evacs_through(FIRST["lat"] + 2 * n)[1])
                TT(latT[:, a_:b_, :], latT[:, a_:b_, :], over_heads(rl[:], b_ - a_), ALU.mult).then_inc(lat_norm, 1)
                dve.wait_ge(lat_hi, due(l, lat_hi, n + 1))
                TT(latl[:, a_:b_, :], latT[:, a_:b_, :], f32(lath[:, a_:b_, :]), ALU.subtract).then_inc(lat_lo, 1)
                if n:
                    dve.wait_ge(kr_mm, due(l, kr_mm, 1))
                    TT(kr[:], side[4][:, S:2 * S], sinT[:], ALU.mult).then_inc(kr_b, 1)
                    TT(kra[:], krx[:], cosT[:], ALU.mult).then_inc(kr_b, 1)
                    dve.wait_ge(kr_b, due(l, kr_b, 2))
                    TT(kr[:], kr[:], kra[:], ALU.add).then_inc(kr_b, 1)
                    dve.wait_ge(kr_b, due(l, kr_b, 3))
                    for e in range(2):
                        TS(krz[:, e, :], kr[:], cst[:, C_FREQ + 2 + e:C_FREQ + 3 + e], None, ALU.mult).then_inc(kr_out, 1)

            def qrope(l, i):
                q_ = qr[:, 2 * i:2 * i + 2, :]
                tmp = sq[i][:].rearrange("p (c s) -> p c s", c=2)
                dve.wait_ge(qr_mm, due(l, qr_mm, i + 1))
                TT(tmp, side[4][:].rearrange("p (c s) -> p c s", c=2), over_heads(sinT[:], 2), ALU.mult).then_inc(qr_b, 1)
                TT(q_, q_, over_heads(cosT[:], 2), ALU.mult).then_inc(qr_b, 1)
                dve.wait_ge(qr_b, due(l, qr_b, 2 * i + 2))
                TT(q_, q_, tmp, ALU.add).then_inc(qr_out, 1)

            def heads4(ap):
                return ap.rearrange("p (e c) -> p e c", e=4)

            def small(slot, t, h0, first=0):
                a_ = 16 * t + first + h0
                return sm[:, slot, a_:a_ + 4]

            def ktrans(l, half):
                dve.wait_ge(ktrans_mm, due(l, ktrans_mm, half + 1))
                dve.wait_ge(gc_exp, due(l, gc_exp, 2))
                TT(ktok[:, 4 * half:4 * half + 4, :], heads4(side[2 + half][:]), along(small(13, 0, 4 * half), P),
                   ALU.mult).then_inc(ktrans_out, 1)

            def decay(l, g):
                b_ = 2 * (g % 2)
                dve.wait_ge(dec_mm, due(l, dec_mm, g + 1))
                dve.wait_ge(dec_exp, due(l, dec_exp, g + 1))
                for e, h in enumerate(heads_of(g)):
                    beta = sm[:, 8, 16 * (g // 2) + 8 + h:16 * (g // 2) + 9 + h]
                    x_ = STT(LT[:, g, e, :], side[b_][:, e * P:(e + 1) * P], beta, DT[:, g, e, :], ALU.mult, ALU.mult)
                x_.then_inc(dec_out, 1)
                TT(AT[:, g], heads4(side[b_ + 1][:]), DT[:, g], ALU.mult).then_inc(dec_out, 1)

            def lvP(l, i):
                lv, g = divmod(i, 4)
                mask = cst[:, C_LV + 64 * lv:C_LV + 64 * (lv + 1)]
                dve.wait_ge(lv_p, due(l, lv_p, i + 1))
                TT(PB[:, g], side[g][:, 0:256].rearrange("p (e c) -> p e c", e=4), over_heads(mask, 4),
                   ALU.mult).then_inc(lv_p_out, 1)

            def lvV(l, i):
                lv, g = divmod(i, 4)
                s = SIZES[lv]
                dve.wait_ge(lv_v, due(l, lv_v, i + 1))
                x_ = X[:, g].rearrange("p e (b two s) -> p (e b) two s", two=2, s=s)[:, :, 0, :]
                TT(x_, x_, side[g][:, 0:256].rearrange("p (b s) -> p b s", s=s), ALU.subtract).then_inc(lv_x, 1)

            def t_v0(l, half):
                dve.wait_ge(t_v0m, due(l, t_v0m, half + 1))
                TT(vn0[:, 4 * half:4 * half + 4, :], heads4(side[half][:]), along(small(8, 0, 4 * half, 8), P),
                   ALU.mult).then_inc(t_v0o, 1)

            def t_v1(l, half):
                dve.wait_ge(t_v1m, due(l, t_v1m, half + 1))
                TT(vn1[:, 4 * half:4 * half + 4, :], heads4(side[2 + half][:]), along(small(8, 1, 4 * half, 8), P),
                   ALU.mult).then_inc(t_v1o, 1)

            def t_ks(l, half):
                hs = slice(4 * half, 4 * half + 4)
                dve.wait_ge(t_ksm, due(l, t_ksm, half + 1))
                TT(rr[:, hs, :], heads4(side[half][:]), along(small(11, 1, 4 * half), P), ALU.mult).then_inc(t_kst, 1)
                dve.wait_ge(t_kst, due(l, t_kst, half + 1))
                TT(rr[:, hs, :], vtok[:, 1, hs, :], rr[:, hs, :], ALU.subtract).then_inc(t_kso, 1)

            def onrm(l, i):
                o_ = oT[:, 2 * i:2 * i + 2, :].rearrange("p c s -> p (c s)")
                dve.wait_ge(on_r, due(l, on_r, 2 * i + 2))
                STT(o_, o_, col(GDN), rn[i % 2][:], ALU.mult, ALU.mult).then_inc(on_o, 1)

            def osplit(l, i):
                p_ = slice(2 * i, 2 * i + 2)
                dve.wait_ge(on_hi, due(l, on_hi, i + 1))
                TT(ol[:, p_, :], oT[:, p_, :], f32(oh[:, p_, :]), ALU.subtract).then_inc(on_lo, 1)

            def sc(l, n):
                qt, hs = unit(n)
                nh, w = len(hs), P * (qt + 1)
                e_ = E[n % 2][:].rearrange("p (e c) -> p e c", e=nh)
                mask = amask[:, P * (1 - qt):2 * P]
                dve.wait_ge(sc_mm, due(l, sc_mm, n + 1))
                if n >= 2:
                    dve.wait_ge(tr_mm, due(l, tr_mm, n - 1))
                TT(e_, side[n % 2][:].rearrange("p (e c) -> p e c", e=nh), over_heads(mask, nh), ALU.add).then_inc(sm_mask, 1)
                dve.wait_ge(sm_mask, due(l, sm_mask, n + 1))
                V.tensor_reduce(mx[:, 0:nh], e_, AX, ALU.max).then_inc(sm_max, 1)
                dve.wait_ge(sm_max, due(l, sm_max, n + 1))
                TT(e_, e_, along(mx[:, 0:nh], w), ALU.subtract).then_inc(sm_sub, 1)
                dve.wait_ge(sm_exp, due(l, sm_exp, n + 1))
                V.tensor_reduce(mx[:, 0:nh], e_, AX, ALU.add).then_inc(sm_sum, 1)
                dve.wait_ge(sm_sum, due(l, sm_sum, n + 1))
                V.reciprocal(rs[:, 0:nh], mx[:, 0:nh]).then_inc(sm_rec, 1)
                dve.wait_ge(sm_rec, due(l, sm_rec, n + 1))
                TT(e_, e_, along(rs[:, 0:nh], w), ALU.mult).then_inc(sm_out, 1)

            def pv(l, n):
                qt, hs = unit(n)
                nh = len(hs)
                dve.wait_ge(pv_hi, due(l, pv_hi, n + 1))
                where = (slice(None), slice(hs[0], hs[0] + nh), slice(qt * P, (qt + 1) * P))
                TT(al[where], side[3 + n % 2][:, 0:nh * P].rearrange("p (e c) -> p e c", e=nh), f32(ah[where]),
                   ALU.subtract).then_inc(pv_lo, 1)

            def job(l, j):
                kind, i, _ = JOBS[j]
                bank = dense[j % 3]
                if kind in EVAC_BY_ACT:
                    return
                dve.wait_ge(steps_done, products_done(l, j))
                pair = slice(2 * (i % 4), 2 * (i % 4) + 2)
                b2 = bank[:].rearrange("p (c s) -> p c s", c=2)
                if kind == "gate":
                    V.tensor_copy(gates[:, i // 4, pair, :], b2).then_inc(dve_evac, 1)
                elif kind == "ya":
                    dve.wait_ge(sig_done, due(l, sig_done, 4))
                    TT(hA[:, pair, :], b2, gates[:, 0, pair, :], ALU.mult).then_inc(dve_evac, 1)
                elif kind == "lat":
                    dve.wait_ge(lat_sq, due(l, lat_sq, i + 1))
                    for c in range(2 if i < 2 else 1):
                        x_ = TS(latT[:, 2 * i + c, :], bank[:, c * S:(c + 1) * S], col(KVA + c if i == 0 else QA + 2 * i - 2 + c),
                                None, ALU.mult)
                    if i == 2:
                        x_ = V.tensor_copy(krx[:], bank[:, S:2 * S])
                    x_.then_inc(dve_evac, 1)
                elif kind in ("out", "ff2"):
                    w = kind == "ff2"
                    dve.wait_ge(y_sq, due(l, y_sq, 4 * w + i + 1))
                    for c in range(2):
                        x_ = TS(yT[:, 2 * i + c, :], bank[:, c * S:(c + 1) * S], col((POST_FFN if w else POST_MIX) + 2 * i + c),
                                None, ALU.mult)
                    x_.then_inc(dve_evac, 1)
                elif kind == "yb":
                    TT(hB[i % 2][:].rearrange("p (c s) -> p c s", c=2), b2, gates[:, 1, pair, :],
                       ALU.mult).then_inc(dve_evac, 1)
                    dve.wait_ge(dve_evac, l * NDVE_EVAC + evacs_through(j)[1])
                    TT(hA[:, pair, :], hA[:, pair, :], hB[i % 2][:].rearrange("p (c s) -> p c s", c=2),
                       ALU.add).then_inc(h_sum, 1)
                elif kind == "ff1":
                    if i == 0:
                        dve.wait_ge(rnorm, due(l, rnorm, 4))
                    STT(fr[i % 4][:].rearrange("p (c s) -> p c s", c=2), b2, 0.0, over_heads(rn[1][:, 0:S], 2), ALU.max,
                        ALU.mult).then_inc(dve_evac, 1)

            def hsplit(l, i):
                p_ = slice(2 * i, 2 * i + 2)
                dve.wait_ge(h_hi, due(l, h_hi, i + 1))
                TT(hl[:, p_, :], hA[:, p_, :], f32(hh[:, p_, :]), ALU.subtract).then_inc(h_lo, 1)

            def post(l, w):
                dve.wait_ge(y_r, due(l, y_r, 2 * w + 2))
                dve.wait_ge(dve_evac, l * NDVE_EVAC + evacs_through(FIRST["ff2" if w else "out"] + 3)[1])

                def times_norm(c):
                    pair = slice(2 * c, 2 * c + 2)
                    TT(yT[:, pair, :], yT[:, pair, :], over_heads(rn[0][:, 0:S], 2), ALU.mult).then_inc(y_scaled, 1)

                def add(c):
                    dve.wait_ge(y_scaled, due(l, y_scaled, 4 * w + c + 1))
                    pair = slice(2 * c, 2 * c + 2)
                    TT(xT[:, pair, :], xT[:, pair, :], yT[:, pair, :], ALU.add).then_inc(x_by_dve, 1)

                def low(c):
                    if w == 0:
                        x_pair = x_by_pool if c % 2 else x_by_dve
                        dve.wait_ge(x_pair, due(l, x_pair, 3 + c // 2))
                        for e in (2 * c, 2 * c + 1):
                            dve.wait_ge(fu_hi, due(l, fu_hi, e + 1))
                            STT(ful[:, e, :], xT[:, e, :], col(PRE_FFN + e), f32(fuh[:, e, :]), ALU.mult,
                                ALU.subtract).then_inc(fu_lo, 1)

                times_norm(0)
                times_norm(1)
                add(0)
                times_norm(2)
                low(0)
                times_norm(3)
                add(2)
                low(1)
                low(2)
                low(3)

            def fsplit(l, i):
                dve.wait_ge(f_hi, due(l, f_hi, i + 1))
                TT(fl[:, 2 * i:2 * i + 2, :], fr[i % 4][:].rearrange("p (c s) -> p c s", c=2),
                   f32(fh[:, 2 * i:2 * i + 2, :]), ALU.subtract).then_inc(f_lo, 1)

            do = dict(start=start, sqsum=sqsum, norm=norm, ab=ab, logits=logits, gc=gc, dt=dt, conv=conv, nrm=nrm, latn=latn, qrope=qrope, ktrans=ktrans,
                      decay=decay, lvP=lvP, lvV=lvV, t_v0=t_v0, t_v1=t_v1, t_ks=t_ks, onrm=onrm, osplit=osplit, sc=sc, pv=pv, job=job,
                      hsplit=hsplit, post=post, fsplit=fsplit)

            V.memset(eps_col, EPS).then_inc(s_trig, 1)
            V.memset(lnscale_col, math.log(DK ** -0.5)).then_inc(s_trig, 1)
            dve.wait_ge(s_tab, 2 * 16)
            n_ = [2]

            def step(ins):
                n_[0] += 1
                ins.then_inc(s_trig, 1)
                dve.wait_ge(s_trig, n_[0])

            turn = 2.0 * math.pi
            t1 = 6.28125
            t2 = round((turn - t1) * 2 ** 22) / 2 ** 22
            t3 = turn - t1 - t2
            magic = 1.5 * 2 ** 23
            A_ = lambda i: ang[:, i, :]
            step(V.tensor_copy(A_(2), pos_i[:]))
            step(TS(A_(2), A_(2), cst[:, C_FREQ:C_FREQ + 1], None, ALU.mult))
            for dst, shift, add in ((0, 0.25, 0.5 * math.pi), (1, 0.0, 0.0)):
                step(TS(A_(3), A_(2), 1.0 / turn, shift, ALU.mult, ALU.add))
                step(TS(A_(3), A_(3), magic, None, ALU.add))
                step(TS(A_(3), A_(3), magic, None, ALU.subtract))
                step(STT(A_(dst), A_(3), -t1, A_(2), ALU.mult, ALU.add))
                step(STT(A_(dst), A_(3), -t2, A_(dst), ALU.mult, ALU.add))
                step(STT(A_(dst), A_(3), -t3, A_(dst), ALU.mult, ALU.add))
                step(TS(A_(dst), A_(dst), add, None, ALU.add))
                step(TS(A_(dst), A_(dst), PI_BELOW, -PI_BELOW, ALU.min, ALU.max))
            dve.wait_ge(s_trig_a, 2)
            step(TS(sinT[:], sinT[:], cst[:, C_FREQ + 1:C_FREQ + 2], None, ALU.mult))
            dve.wait_ge(s_x, 16)
            dve.wait_ge(s_in, 3 * 16)

            with dve.Fori(0, DEPTH) as l:
                for (what, n), pieces in zip(ORDER, splits_at):
                    for p_ in pieces:
                        split_lo(l, p_)
                    if what in do:
                        do[what](l, n)

        @block.gpsimd
        def _(pool):
            G = nc.gpsimd.tensor_tensor

            def nrm(l, i):
                src = [qT, kT][i // 4][:, 2 * (i % 4):2 * (i % 4) + 2, :].rearrange("p c s -> p (c s)")
                pool.wait_ge(silu_done, due(l, silu_done, 5 + i))
                if i >= 2:
                    pool.wait_ge(nrm_mm, due(l, nrm_mm, i - 1))
                G(sq[i % 2][:], src, src, ALU.mult).then_inc(nrm_sq, 1)

            def dt(l, g):
                pool.wait_ge(gc_copied, due(l, gc_copied, 1))
                gc_m = sm[:, 9, 16 * (g // 2) + 4 * (g % 2):16 * (g // 2) + 4 * (g % 2) + 4]
                G(DT[:, g], over_heads(future, 4), along(gc_m, P), ALU.subtract).then_inc(dt_fut, 1)

            def latn(l, n):
                if n == 1:
                    for half in range(2):
                        hs = slice(4 * half, 4 * half + 4)
                        pool.wait_ge(dec_eg, due(l, dec_eg, half + 1))
                        pool.wait_ge(nrm_out, due(l, nrm_out, 4))
                        G(qd[:, hs, :], qT[:, hs, P:2 * P], qd[:, hs, :], ALU.mult).then_inc(qd_out, 1)

            def squares(l, _):
                for c in (0, 4):
                    pool.wait_ge(squared, due(l, squared, 4 + c // 2 + 2))
                    G(fusq[:, c:c + 2, :], fusq[:, c:c + 2, :], fusq[:, c + 2:c + 4, :], ALU.add).then_inc(sq_sum_pool, 1)

            def yadd(l, n):
                pool.wait_ge(y_sq, due(l, y_sq, 4 * (n // 2) + n % 2 + 2))
                if n % 2:
                    pool.wait_ge(y_add, due(l, y_add, n))
                G(sq[0][:], sq[0][:], sq[1][:], ALU.add).then_inc(y_add, 1)

            def x1(l, g):
                pool.wait_ge(dec_out, due(l, dec_out, 2 * g + 2))
                G(XT[:, g], LT[:, g], over_heads(below1, 4), ALU.mult).then_inc(x1_mask, 1)
                pool.wait_ge(x1_mask, due(l, x1_mask, g + 1))
                G(XT[:, g], over_heads(ident, 4), XT[:, g], ALU.subtract).then_inc(x1_xt, 1)

            def onrm(l, i):
                src = oT[:, 2 * i:2 * i + 2, :].rearrange("p c s -> p (c s)")
                pool.wait_ge(t_oo, due(l, t_oo, 2))
                if i >= 2:
                    pool.wait_ge(on_mm, due(l, on_mm, i - 1))
                G(sq[i % 2][:], src, src, ALU.mult).then_inc(on_sq, 1)

            def osplit(l, i):
                o_ = oT[:, 2 * i:2 * i + 2, :].rearrange("p c s -> p (c s)")
                pool.wait_ge(on_o, due(l, on_o, i + 1))
                pool.wait_ge(act_evac, l * NACT_EVAC + evacs_through(FIRST["z"] + 3)[1])
                G(o_, o_, zs[:, 2 * i:2 * i + 2, :].rearrange("p c s -> p (c s)"), ALU.mult).then_inc(on_z, 1)

            def fsplit(l, i):
                pool.wait_ge(dve_evac, l * NDVE_EVAC + evacs_through(FIRST["ff1"] + i)[1])
                G(fr[i % 4][:], fr[i % 4][:], fr[i % 4][:], ALU.mult).then_inc(f_sq, 1)

            def post(l, w):
                for c in (1, 3):
                    pair = slice(2 * c, 2 * c + 2)
                    pool.wait_ge(y_scaled, due(l, y_scaled, 4 * w + c + 1))
                    G(xT[:, pair, :], xT[:, pair, :], yT[:, pair, :], ALU.add).then_inc(x_by_pool, 1)

            do = dict(squares=squares, yadd=yadd, nrm=nrm, dt=dt, latn=latn, x1=x1, onrm=onrm, osplit=osplit, fsplit=fsplit, post=post)
            pool.wait_ge(s_tab, 2 * 16)
            pool.wait_ge(s_x, 16)
            pool.wait_ge(s_in, 3 * 16)
            pool.sem_inc(x_by_pool, 2)
            with pool.Fori(0, DEPTH) as l:
                for what, n in ORDER:
                    if what in do:
                        do[what](l, n)


def constants():
    c = np.zeros((P, NCST), np.float32)
    i = np.arange(P)
    c[:, C_ID:C_ID + P] = np.eye(P)
    c[:, C_UT:C_UT + P] = i[:, None] <= i[None, :]
    c[:, C_NEG:C_NEG + P] = np.where(i[:, None] > i[None, :], -1e30, 0.0)
    c[:, C_M1:C_M1 + P] = (i[None, :] % 2 == 1) & (i[:, None] == i[None, :] - 1)
    for lv, s in enumerate(SIZES):
        pair_of_column = np.arange(64) // s
        c[:, C_LV + 64 * lv:C_LV + 64 * (lv + 1)] = i[:, None] // s == 2 * pair_of_column[None, :] + 1
    c[:, C_ONE:C_ONE + P] = 1.0
    c[:, C_PERM:C_PERM + P] = i[:, None] == (i[None, :] ^ (ROPE // 2))
    c[:, C_AM + P:C_AM + 2 * P] = np.where(i[None, :] // CHUNK > i[:, None] // CHUNK, -1e30, 0.0)
    freq = np.float32(10000.0) ** (-np.arange(0, ROPE, 2, dtype=np.float32) / np.float32(ROPE))
    c[:, C_FREQ] = freq[i % (ROPE // 2)]
    c[:, C_FREQ + 2] = i < ROPE
    c[:, C_FREQ + 3] = i >= ROPE
    c[:, C_FREQ + 1] = np.where(i % ROPE < ROPE // 2, -1.0, 1.0)
    return c


def blocks(w, k0, kn_, cols):
    a = w[k0 * P:(k0 + kn_) * P][:, cols]
    return a.reshape(kn_, P, -1).transpose(1, 0, 2).reshape(P, -1)


def lay_out_weights(w_in, w_uq, w_ukv, w_a, w_b, w_out, w_ff1, w_ff2):
    q0, k0, v0 = 0, H * DK, 2 * H * DK
    z0 = QKV
    cq0 = z0 + H * DK + 2 * H
    ckv0, kr0 = cq0 + QL, cq0 + QL + KVL
    g0 = kr0 + ROPE
    r = np.arange
    pieces = []
    for lyr in range(DEPTH):
        def wide(w, cols, kd=KD):
            for h_ in range(kd // 4):
                pieces.append(blocks(w, 4 * h_, 4, cols))
        for start in (v0, q0, k0):
            for i in range(4):
                wide(w_in[lyr], start + 256 * i + r(256))
        krope = kr0 + r(ROPE)
        wide(w_in[lyr], ckv0 + r(256))
        wide(w_in[lyr], cq0 + r(256))
        wide(w_in[lyr], np.concatenate([cq0 + 256 + r(128), krope, krope]))
        for part in range(2):
            for half in range(2):
                cols = np.concatenate([(4 * half + e) * 2 * DK + part * DK + r(DK) for e in range(4)])
                pieces.append(blocks(w_ukv[lyr], 0, KKV, cols))
        per_head = DK + ROPE
        for i in range(6):
            if i < 4:
                cols = np.concatenate([(2 * i + e) * per_head + r(DK) for e in range(2)])
            else:
                cols = np.concatenate([(4 * (i - 4) + e) * per_head + DK + r(ROPE) for e in range(4)])
            p_ = blocks(w_uq[lyr], 0, KQ, cols)
            pieces.append(np.pad(p_, ((0, 0), (0, PIECE - p_.shape[1]))))
        for start, count in ((z0, 4), (g0, 8)):
            for i in range(count):
                wide(w_in[lyr], start + 256 * i + r(256))
        for w in (w_a, w_b, w_out):
            for i in range(4):
                wide(w[lyr], 256 * i + r(256))
        for i in range(16):
            wide(w_ff1[lyr], 256 * i + r(256))
        for i in range(4):
            wide(w_ff2[lyr], 256 * i + r(256), KF)
    return np.ascontiguousarray(np.stack(pieces))


def lay_out_params(p):
    out = []
    for lyr in range(DEPTH):
        cols = [p[n][lyr].reshape(-1, P).T for n in ("pre_mix_norm_w", "post_mix_norm_w", "pre_ffn_norm_w", "post_ffn_norm_w")]
        cols.append(p["conv_w"][lyr].reshape(-1, P).T)
        cols += [p[n][lyr].reshape(-1, P).T for n in ("q_a_norm_w", "kv_a_norm_w", "gdn_norm_w")]
        cols += [np.broadcast_to(p[n][lyr], (P, H)) for n in ("A_log", "dt_bias")]
        out.append(np.concatenate(cols, axis=1))
    return np.ascontiguousarray(np.stack(out, axis=1))


def kernel(**inputs):
    import concourse.bacc as _bacc
    from concourse.bass_utils import run_bass_kernel_spmd as _run

    a = {k: np.asarray(v) for k, v in inputs.items()}
    ab0 = QKV + H * DK
    arrays = {
        "x_t": np.ascontiguousarray(a["x"][0].T.reshape(KD, P, S).transpose(1, 0, 2)),
        "pos": np.ascontiguousarray(np.broadcast_to(a["positions"][0], (P, S))),
        "weights": lay_out_weights(a["w_in"], a["w_uq"], a["w_ukv"], a["w_branch_a"], a["w_branch_b"], a["w_out"],
                                   a["w_ff1"], a["w_ff2"]),
        "w_ab": np.ascontiguousarray(np.stack([blocks(a["w_in"][i], 0, KD, ab0 + np.arange(16)) for i in range(DEPTH)], axis=1)),
        "params": lay_out_params(a),
        "consts": constants(),
    }
    nc = _bacc.Bacc("TRN2", target_bir_lowering=False, num_devices=1)
    aps = [nc.dram_tensor(n, v.shape, mybir.dt.from_np(v.dtype), kind="ExternalInput").ap() for n, v in arrays.items()]
    out = nc.dram_tensor("out_t", (P, KD, S), F32, kind="ExternalOutput").ap()
    build(nc, *aps, out)
    r = _run(nc, [arrays], core_ids=[0])
    y = np.asarray(r.results[0]["out_t"])
    return np.ascontiguousarray(y.transpose(1, 0, 2).reshape(D, S).T)[None]
```
